# Optimizing a Trainium2 kernel written in Bass

```python
import math
import jax, jax.numpy as jnp
from jax import lax
import numpy as np

D_MODEL = 2048
BATCH = 1
SEQ = 256
DEPTH = 1

HEAD_DIM = 64
ATTN_WIDTH = D_MODEL // 2
RWKV_WIDTH = D_MODEL - ATTN_WIDTH
N_ATTN_HEADS = ATTN_WIDTH // HEAD_DIM
N_RWKV_HEADS = RWKV_WIDTH // HEAD_DIM
DILATED_PATTERNS = ((128, 1), (512, 4), (2048, 16))
REL_BUCKETS = 32
REL_MAX_DIST = 2048
RWKV_DECAY_RANK = max(32, int(round(1.8 * RWKV_WIDTH ** 0.5 / 32)) * 32)
RWKV_A_RANK = max(32, int(round(1.8 * RWKV_WIDTH ** 0.5 / 32)) * 32)
RWKV_GATE_RANK = max(32, int(round(0.6 * RWKV_WIDTH ** 0.8 / 32)) * 32)
RWKV_COLS = 3 * RWKV_WIDTH + RWKV_DECAY_RANK + RWKV_A_RANK + RWKV_GATE_RANK
RWKV_SPLITS = (RWKV_WIDTH, 2 * RWKV_WIDTH, 3 * RWKV_WIDTH,
               3 * RWKV_WIDTH + RWKV_DECAY_RANK,
               3 * RWKV_WIDTH + RWKV_DECAY_RANK + RWKV_A_RANK)
IN_COLS = 3 * ATTN_WIDTH + RWKV_COLS
FFN_HIDDEN = -(-(8 * D_MODEL) // (3 * 256)) * 256
RMS_EPS = 1e-6
GN_EPS = 64e-5
DECAY_SCALE = math.exp(-0.5)
ATTN_SCALE = HEAD_DIM ** -0.5


def rms_norm(x, g):
    xf = x.astype(jnp.float32)
    y = xf * lax.rsqrt(jnp.mean(xf * xf, axis=-1, keepdims=True) + RMS_EPS)
    return (y * g.astype(jnp.float32)).astype(x.dtype)

def t5_bucket(dist):
    exact = REL_BUCKETS // 2
    d_f = jnp.maximum(dist, 1).astype(jnp.float32)
    large = exact + (jnp.log(d_f / exact) / math.log(REL_MAX_DIST / exact)
                     * (REL_BUCKETS - exact)).astype(jnp.int32)
    large = jnp.minimum(large, REL_BUCKETS - 1)
    return jnp.where(dist < exact, dist, large)

def dilated_branch(q, k, v, bias_table, window, dilation):
    b, s, h, dh = q.shape
    blk = window // dilation
    span = blk * dilation
    sp = -(-s // span) * span
    nblk = sp // span

    def blocks(t):
        t = jnp.pad(t, ((0, 0), (0, sp - s), (0, 0), (0, 0)))
        return t.reshape(b, nblk, blk, dilation, h, dh)

    def with_prev(t):
        prev = jnp.pad(t, ((0, 0), (1, 0), (0, 0), (0, 0), (0, 0), (0, 0)))[:, :-1]
        return jnp.concatenate([prev, t], axis=2)

    qb = blocks(q)
    kc = with_prev(blocks(k))
    vc = with_prev(blocks(v))
    qi = jnp.arange(blk)[:, None]
    ki = jnp.arange(2 * blk)[None, :]
    rel = qi + blk - ki
    band = (rel >= 0) & (rel <= blk)
    bias = bias_table[t5_bucket(jnp.clip(rel, 0, blk) * dilation)]
    bias = jnp.transpose(bias, (2, 0, 1)).astype(jnp.float32)
    not_first = jnp.arange(nblk)[:, None, None] > 0
    valid = band[None] & (not_first | (ki >= blk)[None])
    logits = jnp.einsum('bnqrhd,bnkrhd->bnrhqk', qb, kc) * ATTN_SCALE + bias
    logits = jnp.where(valid[None, :, None, None], logits, -jnp.inf)
    m = jnp.max(logits, axis=-1, keepdims=True)
    p = jnp.exp(logits - m)
    l = jnp.sum(p, axis=-1, keepdims=True)
    o = jnp.einsum('bnrhqk,bnkrhd->bnqrhd', p / l, vc)
    lse = (m + jnp.log(l))[..., 0]
    o = o.reshape(b, sp, h, dh)[:, :s]
    lse = jnp.transpose(lse, (0, 1, 4, 2, 3)).reshape(b, sp, h)[:, :s]
    return o, lse

def dilated_attention(q, k, v, bias_table):
    outs, lses = [], []
    for window, dilation in DILATED_PATTERNS:
        o, lse = dilated_branch(q, k, v, bias_table, window, dilation)
        outs.append(o)
        lses.append(lse)
    wts = jax.nn.softmax(jnp.stack(lses), axis=0)
    return jnp.sum(wts[..., None] * jnp.stack(outs), axis=0)

def rwkv7_step(state, inp):
    r, w, k, v, a, bb = inp
    sa = jnp.einsum('bhij,bhj->bhi', state, a)
    state = (state * w[:, :, None, :] + sa[..., None] * bb[:, :, None, :]
             + v[..., None] * k[:, :, None, :])
    y = jnp.einsum('bhij,bhj->bhi', state, r)
    return state, y

def rwkv7_time_mix(z, shift_mix, w0, w_up, a0, a_up, g_up, k_k, k_a, r_k, ln_w, ln_b):
    b, s, _ = z.shape
    prev = jnp.pad(z, ((0, 0), (1, 0), (0, 0)))[:, :-1]
    z = z + (prev - z) * shift_mix
    r, k, v, w_lo, a_lo, g_lo = jnp.split(z, list(RWKV_SPLITS), axis=-1)
    decay = jnp.exp(-DECAY_SCALE * jax.nn.sigmoid(w0 + jnp.tanh(w_lo) @ w_up))
    a = jax.nn.sigmoid(a0 + a_lo @ a_up)
    g = jax.nn.sigmoid(g_lo) @ g_up

    def heads(t):
        return t.reshape(b, s, N_RWKV_HEADS, HEAD_DIM)

    kk = heads(k * k_k)
    kk = kk / jnp.maximum(jnp.sqrt(jnp.sum(kk * kk, axis=-1, keepdims=True)), 1e-12)
    k = k * (1.0 + (a - 1.0) * k_a)
    rh, kh, vh, wh, ah = heads(r), heads(k), heads(v), heads(decay), heads(a)
    xs = tuple(jnp.moveaxis(t, 1, 0) for t in (rh, wh, kh, vh, -kk, kk * ah))
    state0 = jnp.zeros((b, N_RWKV_HEADS, HEAD_DIM, HEAD_DIM), jnp.float32)
    _, y = lax.scan(rwkv7_step, state0, xs)
    y = jnp.moveaxis(y, 0, 1)
    mu = jnp.mean(y, axis=-1, keepdims=True)
    var = jnp.mean(jnp.square(y - mu), axis=-1, keepdims=True)
    y = ((y - mu) * lax.rsqrt(var + GN_EPS)).reshape(b, s, RWKV_WIDTH) * ln_w + ln_b
    bonus = jnp.sum(rh * kh * r_k, axis=-1, keepdims=True) * vh
    return (y + bonus.reshape(b, s, RWKV_WIDTH)) * g

def first_inputs(seed: int = 0) -> dict:
    key = jax.random.key(seed)
    ks = jax.random.split(key, 20)
    L = DEPTH

    def nrm(k, shape, scale):
        return scale * jax.random.normal(k, shape, jnp.float32)

    return {
        'x': nrm(ks[0], (BATCH, SEQ, D_MODEL), 1.0),
        'norm1_g': 1.0 + nrm(ks[1], (L, D_MODEL), 0.05),
        'w_in': nrm(ks[2], (L, D_MODEL, IN_COLS), D_MODEL ** -0.5),
        'rwkv_shift_mix': jax.random.uniform(ks[3], (L, RWKV_COLS), jnp.float32),
        'rwkv_w0': jnp.linspace(-4.0, 2.0, RWKV_WIDTH, dtype=jnp.float32) + nrm(ks[4], (L, RWKV_WIDTH), 0.1),
        'rwkv_w_up': nrm(ks[5], (L, RWKV_DECAY_RANK, RWKV_WIDTH), 0.5 * RWKV_DECAY_RANK ** -0.5),
        'rwkv_a0': nrm(ks[6], (L, RWKV_WIDTH), 0.1),
        'rwkv_a_up': nrm(ks[7], (L, RWKV_A_RANK, RWKV_WIDTH), RWKV_A_RANK ** -0.5),
        'rwkv_g_up': nrm(ks[8], (L, RWKV_GATE_RANK, RWKV_WIDTH), RWKV_GATE_RANK ** -0.5),
        'rwkv_k_k': 0.85 + nrm(ks[9], (L, RWKV_WIDTH), 0.05),
        'rwkv_k_a': 1.0 + nrm(ks[10], (L, RWKV_WIDTH), 0.05),
        'rwkv_r_k': nrm(ks[11], (L, N_RWKV_HEADS, HEAD_DIM), 0.1),
        'rwkv_ln_w': 1.0 + nrm(ks[12], (L, RWKV_WIDTH), 0.05),
        'rwkv_ln_b': nrm(ks[13], (L, RWKV_WIDTH), 0.02),
        'rel_bias_table': nrm(ks[14], (REL_BUCKETS, N_ATTN_HEADS), 0.5),
        'w_out': nrm(ks[15], (L, D_MODEL, D_MODEL), D_MODEL ** -0.5),
        'norm2_g': 1.0 + nrm(ks[16], (L, D_MODEL), 0.05),
        'w_gate_up': nrm(ks[17], (L, D_MODEL, 2 * FFN_HIDDEN), D_MODEL ** -0.5),
        'w_down': nrm(ks[18], (L, FFN_HIDDEN, D_MODEL), FFN_HIDDEN ** -0.5),
        'final_g': 1.0 + nrm(ks[19], (D_MODEL,), 0.05),
    }

def first_block(x, norm1_g, w_in, rwkv_shift_mix, rwkv_w0, rwkv_w_up, rwkv_a0, rwkv_a_up,
              rwkv_g_up, rwkv_k_k, rwkv_k_a, rwkv_r_k, rwkv_ln_w, rwkv_ln_b, rel_bias_table,
              w_out, norm2_g, w_gate_up, w_down, final_g):
    b, s, _ = x.shape
    h = x
    for l in range(DEPTH):
        u = rms_norm(h, norm1_g[l])
        proj = (u @ w_in[l]).astype(jnp.float32)
        q, k, v, z = jnp.split(proj, [ATTN_WIDTH, 2 * ATTN_WIDTH, 3 * ATTN_WIDTH], axis=-1)
        hd = (b, s, N_ATTN_HEADS, HEAD_DIM)
        attn = dilated_attention(q.reshape(hd), k.reshape(hd), v.reshape(hd),
                                 rel_bias_table.astype(jnp.float32))
        rw = rwkv7_time_mix(z, rwkv_shift_mix[l], rwkv_w0[l], rwkv_w_up[l], rwkv_a0[l],
                            rwkv_a_up[l], rwkv_g_up[l], rwkv_k_k[l], rwkv_k_a[l],
                            rwkv_r_k[l], rwkv_ln_w[l], rwkv_ln_b[l])
        mixed = jnp.concatenate([attn.reshape(b, s, ATTN_WIDTH), rw], axis=-1).astype(h.dtype)
        h = h + mixed @ w_out[l]
        u = rms_norm(h, norm2_g[l])
        gate, up = jnp.split(u @ w_gate_up[l], 2, axis=-1)
        h = h + (jax.nn.silu(gate) * up) @ w_down[l]
    return rms_norm(h, final_g)


D_MIX = D_MODEL
CONV_CH = D_MIX // 2
N_Q_HEADS = (D_MIX - CONV_CH) // HEAD_DIM
N_KV_HEADS = 2
GQA_GROUP = N_Q_HEADS // N_KV_HEADS
ATTN_CH = N_Q_HEADS * HEAD_DIM
KV_CH = N_KV_HEADS * HEAD_DIM
IN_COLS_2 = 2 * CONV_CH + ATTN_CH + 2 * KV_CH
CONV_K = 31
WINDOW = 128
BLOCK = 128
ROT_DIM = HEAD_DIM // 4
ROPE_THETA = 500000.0
EPS = 1e-6
N_KEYS = 128
N_EXPERTS = N_KEYS * N_KEYS
PEER_HEADS = 8
PEER_KEY_DIM = 256
PEER_HALF = PEER_KEY_DIM // 2
PEER_TOPK = 16
PEER_CHUNK = 128


def rms_norm_2(x, g):
    xf = x.astype(jnp.float32)
    y = xf * lax.rsqrt(jnp.mean(xf * xf, axis=-1, keepdims=True) + EPS)
    return (y * g.astype(jnp.float32)).astype(x.dtype)

def layer_norm(x, g, b):
    xf = x.astype(jnp.float32)
    mu = jnp.mean(xf, axis=-1, keepdims=True)
    var = jnp.mean(jnp.square(xf - mu), axis=-1, keepdims=True)
    y = (xf - mu) * lax.rsqrt(var + EPS)
    return (y * g.astype(jnp.float32) + b.astype(jnp.float32)).astype(x.dtype)

def partial_rotary(t, cos, sin):
    half = ROT_DIM // 2
    r1 = t[..., :half]
    r2 = t[..., half:ROT_DIM]
    return jnp.concatenate([r1 * cos - r2 * sin, r2 * cos + r1 * sin, t[..., ROT_DIM:]], axis=-1)

def conv_group(u, conv_dw_w, conv_dw_b, conv_ln_g, conv_ln_b):
    a, gate = jnp.split(u, 2, axis=-1)
    h = a * jax.nn.sigmoid(gate)
    h = lax.conv_general_dilated(
        h, conv_dw_w[:, None, :].astype(h.dtype), window_strides=(1,),
        padding=[(CONV_K - 1, 0)], dimension_numbers=("NWC", "WIO", "NWC"),
        feature_group_count=CONV_CH) + conv_dw_b
    h = layer_norm(h, conv_ln_g, conv_ln_b)
    return jax.nn.silu(h)

def swa_group(q, k, v, positions, q_norm_g, k_norm_g, attn_sinks):
    B, S, _ = q.shape
    nb = S // BLOCK
    q = rms_norm_2(q.reshape(B, S, N_Q_HEADS, HEAD_DIM), q_norm_g)
    k = rms_norm_2(k.reshape(B, S, N_KV_HEADS, HEAD_DIM), k_norm_g)
    v = v.reshape(B, S, N_KV_HEADS, HEAD_DIM)
    inv_freq = ROPE_THETA ** (-jnp.arange(0, ROT_DIM, 2, dtype=jnp.float32) / ROT_DIM)
    ang = positions.astype(jnp.float32)[..., None] * inv_freq
    cos = jnp.cos(ang)[:, :, None, :].astype(q.dtype)
    sin = jnp.sin(ang)[:, :, None, :].astype(q.dtype)
    q = partial_rotary(q, cos, sin)
    k = partial_rotary(k, cos, sin)

    qb = q.reshape(B, nb, BLOCK, N_KV_HEADS, GQA_GROUP, HEAD_DIM)
    pad = ((0, 0), (BLOCK, 0), (0, 0), (0, 0))
    kb = jnp.pad(k, pad).reshape(B, nb + 1, BLOCK, N_KV_HEADS, HEAD_DIM)
    vb = jnp.pad(v, pad).reshape(B, nb + 1, BLOCK, N_KV_HEADS, HEAD_DIM)
    k_band = jnp.concatenate([kb[:, :-1], kb[:, 1:]], axis=2)
    v_band = jnp.concatenate([vb[:, :-1], vb[:, 1:]], axis=2)

    scores = jnp.einsum("bnqhgd,bnshd->bnhgqs", qb, k_band).astype(jnp.float32)
    scores = scores * (1.0 / math.sqrt(HEAD_DIM))
    blk = jnp.arange(nb)[:, None, None]
    qpos = blk * BLOCK + jnp.arange(BLOCK)[None, :, None]
    kpos = (blk - 1) * BLOCK + jnp.arange(2 * BLOCK)[None, None, :]
    mask = (kpos <= qpos) & (qpos - kpos < WINDOW) & (kpos >= 0)
    scores = jnp.where(mask[None, :, None, None], scores, -1e30)

    sink = attn_sinks.astype(jnp.float32).reshape(1, 1, N_KV_HEADS, GQA_GROUP, 1, 1)
    m = jnp.maximum(jnp.max(scores, axis=-1, keepdims=True), sink)
    p = jnp.exp(scores - m)
    denom = jnp.sum(p, axis=-1, keepdims=True) + jnp.exp(sink - m)
    probs = (p / denom).astype(v.dtype)
    out = jnp.einsum("bnhgqs,bnshd->bnqhgd", probs, v_band)
    return out.reshape(B, S, ATTN_CH)

def peer(xn, peer_w_q, peer_sub_keys, peer_u, peer_v):
    B, S, D = xn.shape
    T = B * S
    xt = xn.reshape(T, D)
    qh = (xt @ peer_w_q).reshape(T, PEER_HEADS, 2, PEER_HALF)
    sub = jnp.einsum("thpc,hpnc->thpn", qh, peer_sub_keys).astype(jnp.float32)
    v1, i1 = lax.top_k(sub[:, :, 0], PEER_TOPK)
    v2, i2 = lax.top_k(sub[:, :, 1], PEER_TOPK)
    cand = (v1[..., :, None] + v2[..., None, :]).reshape(T, PEER_HEADS, PEER_TOPK * PEER_TOPK)
    vals, cidx = lax.top_k(cand, PEER_TOPK)
    e1 = jnp.take_along_axis(i1, cidx // PEER_TOPK, axis=-1)
    e2 = jnp.take_along_axis(i2, cidx % PEER_TOPK, axis=-1)
    experts = e1 * N_KEYS + e2
    gates = jax.nn.softmax(vals, axis=-1).astype(xn.dtype)

    nc = T // PEER_CHUNK

    def chunk_fn(args):
        xc, ec, gc = args
        u_sel = jnp.take(peer_u, ec, axis=0)
        h = jnp.einsum("cd,chkd->chk", xc, u_sel)
        a = jax.nn.gelu(h, approximate=False) * gc
        v_sel = jnp.take(peer_v, ec, axis=0)
        return jnp.einsum("chk,chkd->cd", a, v_sel)

    y = lax.map(chunk_fn, (xt.reshape(nc, PEER_CHUNK, D),
                           experts.reshape(nc, PEER_CHUNK, PEER_HEADS, PEER_TOPK),
                           gates.reshape(nc, PEER_CHUNK, PEER_HEADS, PEER_TOPK)))
    return y.reshape(B, S, D)

def second_inputs(seed: int = 0) -> dict:
    key = jax.random.key(seed)
    ks = jax.random.split(key, 20)
    f32 = jnp.float32
    nrm = lambda k, shape, s: jax.random.normal(k, shape, f32) * s
    positions = jnp.broadcast_to(jnp.arange(SEQ, dtype=jnp.int32)[None, :], (BATCH, SEQ))
    return {
        "x": nrm(ks[0], (BATCH, SEQ, D_MODEL), 1.0),
        "positions": positions,
        "norm1_g": 1.0 + nrm(ks[1], (D_MODEL,), 0.02),
        "w_in": nrm(ks[2], (D_MODEL, IN_COLS_2), D_MODEL ** -0.5),
        "b_in": nrm(ks[3], (IN_COLS_2,), 0.02),
        "conv_dw_w": nrm(ks[4], (CONV_K, CONV_CH), CONV_K ** -0.5),
        "conv_dw_b": nrm(ks[5], (CONV_CH,), 0.02),
        "conv_ln_g": 1.0 + nrm(ks[6], (CONV_CH,), 0.02),
        "conv_ln_b": nrm(ks[7], (CONV_CH,), 0.02),
        "q_norm_g": 1.0 + nrm(ks[8], (HEAD_DIM,), 0.02),
        "k_norm_g": 1.0 + nrm(ks[9], (HEAD_DIM,), 0.02),
        "attn_sinks": nrm(ks[10], (N_Q_HEADS,), 0.5),
        "w_out": nrm(ks[11], (D_MIX, D_MODEL), D_MIX ** -0.5),
        "norm2_g": 1.0 + nrm(ks[12], (D_MODEL,), 0.02),
        "peer_w_q": nrm(ks[13], (D_MODEL, PEER_HEADS * PEER_KEY_DIM), D_MODEL ** -0.5),
        "peer_sub_keys": nrm(ks[14], (PEER_HEADS, 2, N_KEYS, PEER_HALF), PEER_HALF ** -0.5),
        "peer_u": nrm(ks[15], (N_EXPERTS, D_MODEL), D_MODEL ** -0.5),
        "peer_v": nrm(ks[16], (N_EXPERTS, D_MODEL), PEER_HEADS ** -0.5),
    }

def second_block(x, positions, norm1_g, w_in, b_in, conv_dw_w, conv_dw_b, conv_ln_g, conv_ln_b,
              q_norm_g, k_norm_g, attn_sinks, w_out, norm2_g, peer_w_q, peer_sub_keys,
              peer_u, peer_v):
    for _ in range(DEPTH):
        xn = rms_norm_2(x, norm1_g)
        proj = xn @ w_in + b_in
        c0 = 2 * CONV_CH
        conv_in = proj[..., :c0]
        q = proj[..., c0:c0 + ATTN_CH]
        k = proj[..., c0 + ATTN_CH:c0 + ATTN_CH + KV_CH]
        v = proj[..., c0 + ATTN_CH + KV_CH:]
        conv_out = conv_group(conv_in, conv_dw_w, conv_dw_b, conv_ln_g, conv_ln_b)
        attn_out = swa_group(q, k, v, positions, q_norm_g, k_norm_g, attn_sinks)
        mixed = jnp.concatenate([conv_out, attn_out], axis=-1)
        x = x + mixed @ w_out
        x = x + peer(rms_norm_2(x, norm2_g), peer_w_q, peer_sub_keys, peer_u, peer_v)
    return x


def setup_inputs(seed=0):
    out = dict(first_inputs(seed))
    for name, value in second_inputs(seed + 1).items():
        if name != "x":
            out[name + "_2"] = value
    return out


def reference(
    x, norm1_g, w_in, rwkv_shift_mix, rwkv_w0, rwkv_w_up, rwkv_a0, rwkv_a_up, rwkv_g_up,
    rwkv_k_k, rwkv_k_a, rwkv_r_k, rwkv_ln_w, rwkv_ln_b, rel_bias_table, w_out, norm2_g,
    w_gate_up, w_down, final_g, positions_2, norm1_g_2, w_in_2, b_in_2, conv_dw_w_2,
    conv_dw_b_2, conv_ln_g_2, conv_ln_b_2, q_norm_g_2, k_norm_g_2, attn_sinks_2, w_out_2,
    norm2_g_2, peer_w_q_2, peer_sub_keys_2, peer_u_2, peer_v_2,
):
    x = first_block(
        x, norm1_g, w_in, rwkv_shift_mix, rwkv_w0, rwkv_w_up, rwkv_a0, rwkv_a_up, rwkv_g_up,
        rwkv_k_k, rwkv_k_a, rwkv_r_k, rwkv_ln_w, rwkv_ln_b, rel_bias_table, w_out, norm2_g,
        w_gate_up, w_down, final_g,
    )
    return second_block(
        x, positions_2, norm1_g_2, w_in_2, b_in_2, conv_dw_w_2, conv_dw_b_2, conv_ln_g_2,
        conv_ln_b_2, q_norm_g_2, k_norm_g_2, attn_sinks_2, w_out_2, norm2_g_2, peer_w_q_2,
        peer_sub_keys_2, peer_u_2, peer_v_2,
    )


_drawn_inputs = setup_inputs


def setup_inputs(seed=0):
    import zlib

    import numpy as np

    out = dict(_drawn_inputs(seed))
    spreads = {}
    factors = {'rwkv_k_k': 3.396,
     'rwkv_ln_b': 2.799,
     'norm1_g_2': 2.803,
     'conv_ln_g_2': 12.751,
     'conv_ln_b_2': 12.351,
     'q_norm_g_2': 7.079,
     'k_norm_g_2': 7.256,
     'attn_sinks_2': 195.74,
     'conv_dw_b_2': 5.81,
     'norm2_g_2': 5.511}
    for name, (base, spread) in spreads.items():
        noise = np.random.default_rng([zlib.crc32(name.encode()), seed]).standard_normal(out[name].shape)
        drawn = base * np.exp(spread * noise) if base else spread * noise
        out[name] = __import__('jax').numpy.asarray(drawn.astype(out[name].dtype))
    for name, factor in factors.items():
        out[name] = (out[name] * factor).astype(out[name].dtype)
    return out
```

```python
import math
from contextlib import ExitStack

import numpy as np

import concourse.bass as bass
from concourse import mybir

F32 = mybir.dt.float32
I32 = mybir.dt.int32
U32 = mybir.dt.uint32
ALU = mybir.AluOpType
ACT = mybir.ActivationFunctionType
AX = mybir.AxisListType.X

P = 128
T = 256
D = 2048
DT = D // P
HD = 64
NH = 16
W = 1024
WT = W // P
FFN = 5632
FT = FFN // P
RING = 4
SLOT = DT * P
CH = 64
NC_ = T // CH
CONV_K = 31
NK = 128
PH = 8
TOPK = 16
RMS_EPS = 1e-6
GN_EPS = 64e-5
DECAY = math.exp(-0.5)
NEG = -1e30

STAGES = [("qkv", 24), ("z", 27), ("out", 16), ("gu", 88), ("down", 64), ("in2", 26), ("out2", 16),
          ("wq", 16), ("u", 128), ("v", 128)]
BASE = {}
_at = 0
for _name, _n in STAGES:
    BASE[_name] = _at
    _at += _n
DOWN_KT = 11

PARAMS = [("n1", 16), ("n2", 16), ("fg", 16), ("n1b", 16), ("n2b", 16), ("mix", 27), ("w0", 8), ("a0", 8),
          ("kk", 8), ("ka", 8), ("rk", 8), ("lnw", 8), ("lnb", 8), ("bin2", 26), ("cw", 8 * CONV_K), ("cb", 8),
          ("clg", 8), ("clb", 8), ("qg", 1), ("kg", 1)]
PAR = {}
_at = 0
for _name, _n in PARAMS:
    PAR[_name] = (_at, _n)
    _at += _n
NPAR = _at

CONSTS = [("ident", P), ("ones", P), ("blk", P), ("iota", P), ("cmask", P), ("reset", T),
          ("dmask", CH), ("omask", CH), ("dtmask", CH), ("i64", CH), ("swa", 384), ("perm", P), ("invf", 1)]
CON = {}
_at = 0
for _name, _n in CONSTS:
    CON[_name] = (_at, _n)
    _at += _n
NCON = _at
KEEP = 4 * P


def constants():
    p = np.arange(P)[:, None]
    f = np.arange(P)[None, :]
    c = {}
    c["ident"] = p == f
    c["ones"] = np.ones((P, P))
    c["blk"] = (p // HD) == (f // HD)
    c["iota"] = np.broadcast_to(f, (P, P))
    s, t = p % CH, f % CH
    c["cmask"] = np.where(f < CH, s < t, s <= t)
    c["reset"] = np.broadcast_to(np.arange(T)[None, :] % CH != 0, (P, T))
    pp, ff = p, np.arange(CH)[None, :]
    same = (pp % CH) // 16 == ff // 16
    c["dmask"] = (pp % CH < ff) & same
    c["omask"] = (pp % CH < ff) & ~same
    c["dtmask"] = (pp % CH > ff) & same
    c["i64"] = pp % CH == ff
    prev = np.where(f > p, 0.0, NEG)
    diag = np.where(f <= p, 0.0, NEG)
    c["swa"] = np.concatenate([prev, diag, diag], 1)
    perm = np.zeros((P, P))
    for h in (0, HD):
        for i in range(8):
            perm[h + 8 + i, h + i] = -1.0
            perm[h + i, h + 8 + i] = 1.0
    c["perm"] = perm
    inv = np.float32(500000.0) ** (-np.arange(0, 16, 2, dtype=np.float32) / np.float32(16))
    invf = np.zeros((P, 1))
    for h in (0, HD):
        invf[h:h + 8, 0] = inv
        invf[h + 8:h + 16, 0] = inv
    c["invf"] = invf
    return np.concatenate([np.broadcast_to(c[n], (P, k)).astype(np.float32) for n, k in CONSTS], 1)


def distance_constants():
    y = np.arange(384)
    d = 255 - y
    df = np.maximum(d, 1).astype(np.float32)
    large = 16 + (np.log(df / np.float32(16)) / np.float32(math.log(2048 / 16)) * np.float32(16)).astype(np.int32)
    bucket = np.where(d < 16, d, np.minimum(large, 31))
    hot = (np.arange(32)[:, None] == bucket[None, :]) & (d >= 0)[None, :]
    n = (d <= 128).astype(int) + (d % 4 == 0) + (d % 16 == 0)
    n = np.where(d >= 0, n, 0)
    ln = np.where(n > 0, np.log(np.maximum(n, 1)), NEG)
    return np.concatenate([hot.astype(np.float32), np.broadcast_to(ln, (16, 384)).astype(np.float32)], 0)


INVERSE = [
    [(1, 0, 0, [("act", 4)]),
     (0, 1, 1, [("act", 5), ("dve+", 6)])],
    [(5, 4, 2, [("act", 0)]),
     (4, 5, 3, [("act", 1), ("dve+", 3)]),
     (6, 3, 0, [("dve", 7)])],
    [(0, 1, 1, [("dve", 4)]),
     (3, 7, 2, [("act", 5)])],
    [(4, 5, 3, [("act", 0)])],
    [(0, "i", 0, [("dve", 1)])],
    [(1, 2, 1, [("act", 3)]),
     (2, 1, 2, [("act", 4), ("dve+", 6)])],
    [(3, 4, 3, [("dve", 5)])],
    [(5, 0, 0, [("act", 7)])],
    [(6, 7, 1, [("dve", 8)])],
]
PLUS_ID = {(2, 4), (6, 5)}
NSTEP = len(INVERSE)


def evacuations(engine):
    counts = [0]
    for step in INVERSE:
        counts.append(counts[-1] + sum(e.startswith(engine) for _, _, _, ev in step for e, _ in ev))
    return counts


EVA, EVD = evacuations("act"), evacuations("dve")


def build(nc, A):
    ctx = ExitStack()
    with ctx:
        def sem(name):
            return ctx.enter_context(nc.semaphore(name))

        xT = ctx.enter_context(nc.sbuf_tensor("xT", [P, DT, T], F32))
        uT = ctx.enter_context(nc.sbuf_tensor("uT", [P, DT, T], F32))
        ring = ctx.enter_context(nc.sbuf_tensor("ring", [P, RING, SLOT], F32))
        par = ctx.enter_context(nc.sbuf_tensor("params", [P, NPAR], F32))
        con = ctx.enter_context(nc.sbuf_tensor("consts", [P, KEEP], F32))
        misc = ctx.enter_context(nc.sbuf_tensor("misc", [P, 3072], F32))
        arena = ctx.enter_context(nc.sbuf_tensor("arena", [P, 32768], F32))
        ps = ctx.enter_context(nc.psum_tensor("ps", [P, 8, 512], F32))
        dist_dram = nc.dram_tensor("dist_dram", [NH, P, 384], F32).ap()

        def view(tensor, at, *shape):
            n = int(np.prod(shape))
            v = tensor[:, at:at + n]
            if len(shape) == 2:
                return v.rearrange("p (a b) -> p a b", a=shape[0])
            if len(shape) == 3:
                return v.rearrange("p (a b c) -> p a b c", a=shape[0], b=shape[1])
            if len(shape) == 4:
                return v.rearrange("p (a b c d) -> p a b c d", a=shape[0], b=shape[1], c=shape[2])
            return v

        def bank(b):
            return ps[:, b, :]

        def prm(name, i=0):
            return par[:, PAR[name][0] + i:PAR[name][0] + i + 1]

        def cst(name):
            at, n = CON[name]
            return con[:, at:at + n] if at < KEEP else arena[:, at - KEEP:at - KEEP + n]

        ident, ones, blk = cst("ident"), cst("ones"), cst("blk")
        TAIL = NCON - KEEP
        rstd = misc[:, 0:T]
        nrm = misc[:, T:2 * T]

        o = TAIL
        QK = view(arena, o, 16, T); o += 16 * T
        VN = view(arena, o, 2, W); o += 2 * W
        BC = view(arena, o, 2, 384); o += 768
        LG = view(arena, o, 2, 384); o += 768
        PT = view(arena, o, 2, 384); o += 768
        lo = view(arena, o, 3, T); o += 3 * T
        zraw = view(arena, o, 2, T + 1); o += 2 * (T + 1)
        zdif = view(arena, o, T); o += T
        sc = view(arena, o, 12, T); o += 12 * T
        wend = view(arena, o, WT, NC_); o += WT * NC_
        wendh = view(arena, o, NH, NC_); o += NH * NC_
        attn_end = o
        mixT = view(arena, o, DT, T); o += DT * T
        AR = view(arena, o, WT, NC_, P); o += WT * NC_ * P
        BK = view(arena, o, WT, NC_, P); o += WT * NC_ * P
        vT = view(arena, o, WT, T); o += WT * T
        gT = view(arena, o, WT, T); o += WT * T
        LR = view(arena, o, 2, W); o += 2 * W
        LR2 = misc[:, 1408:1408 + W]
        small = misc[:, 2432:2560]
        assert o <= 32768, o
        o = TAIL
        QS = view(arena, o, NH, P); o += NH * P
        MB = view(arena, o, NH, P); o += NH * P
        SV = view(arena, o, NH, CH); o += NH * CH
        UV = view(arena, o, NH, CH); o += NH * CH
        BKn = view(arena, o, NH, CH); o += NH * CH
        Bf = [view(arena, o + 512 * i, 8, CH) for i in range(9)]; o += 9 * 512
        assert o <= attn_end - WT * NC_ - NH * NC_, (o, attn_end)
        yv = BK[:, :, :, 0:CH]
        bonT = mixT[:, WT:DT, :]

        GT = view(arena, TAIL + DT * T, FT, T)
        GS = view(misc, 1024, 2, T)

        o = TAIL
        mix2 = view(arena, o, DT, T); o += DT * T
        PAD = CONV_K - 1
        HP = view(arena, o, WT, T + PAD); o += WT * (T + PAD)
        HS = view(arena, o - WT * (T + PAD), WT, T)
        QR = view(arena, o, WT, T); o += WT * T
        KR = view(arena, o, T); o += T
        VB = view(arena, o, 2, P); o += 2 * P
        LG2 = view(arena, o, 2, 384); o += 768
        PT2 = view(arena, o, 2, 384); o += 768
        sg = view(arena, o, 2, T); o += 2 * T
        qraw = view(arena, o, 2, T); o += 2 * T
        qsq = view(arena, o, 2, T); o += 2 * T
        qnm = view(arena, o, 2, T); o += 2 * T
        qsc = view(arena, o, 4, T); o += 4 * T
        assert o <= 16640, o
        o = 16640
        KEYS = view(arena, o, 2 * PH * NK); o += 2 * PH * NK
        HQ = view(arena, o, DT, T); o += DT * T
        SUB = view(arena, o, 2, 2 * PH, NK); o += 2 * 2 * PH * NK
        posf = view(arena, o, T); o += T
        cosT = view(arena, o, T); o += T
        sinT = view(arena, o, T); o += T
        ropt = view(arena, o, 2, T); o += 2 * T
        sinkr = view(arena, o, NH); o += NH
        bvr = view(arena, o, P); o += P
        exs = view(arena, o, 2, 3, P); o += 6 * P
        pick = view(arena, o, 2, TOPK, TOPK); o += 2 * TOPK * TOPK
        assert o <= 32768, o
        o = 16640 + 2 * PH * NK
        wk = view(arena, o, 2, T); o += 2 * T
        cand = view(arena, o, 2, T); o += 2 * T
        top = view(arena, o, 2, 2 * PH, TOPK); o += 2 * 2 * PH * TOPK
        topi = view(arena, o, 2, 2 * PH, TOPK); o += 2 * 2 * PH * TOPK
        topif = view(arena, o, 2, 2 * PH, TOPK); o += 2 * 2 * PH * TOPK
        val = view(arena, o, 2, PH, TOPK); o += 2 * PH * TOPK
        vali = view(arena, o, 2, 2, PH, TOPK); o += 4 * PH * TOPK
        valf = view(arena, o, 2, 2, PH, TOPK); o += 4 * PH * TOPK
        vsum = view(arena, o, 2, 2 * PH); o += 4 * PH
        assert o <= 16640 + 2 * PH * NK + DT * T, o
        HB = view(arena, 0, NK, T)
        eT = view(misc, 0, 3, T)
        OH = view(misc, 3 * T, 2, 2, 4, P)
        CONV_TILES, Q0 = 16, BASE["in2"] + 16

        s_keys, s_pos, s_sink, s_bv, s_y = (sem(n) for n in ("keys_in", "pos_in", "sinks_in", "bv_in", "y_out"))
        (sg_ready, cv_ev, tap, hp_zero, rope_ready, sin_in, sin_out, q_raw, q_ss, q_rc, q_rt, q_nm, q_rot, q_done,
         v_ev, sc2_ps, lg2_used, lg2_ready, ex2_ready, pn2_ready, tp2_ps, pt2_ready, o2_ps, o2_ev, ln_ps, ln_mid,
         ln_sq, ln_rc, ln_rt, ln_mul, ln_out, wq_ev, sub_ps, sub_ev, u_ev, soft_in, soft_ex, route_ready, et_ps,
         et_ev, oh_ready, g_ps, g_used, seed_ps, y_ready, y_last) = (sem(n) for n in (
            "sg_ready", "conv_in_ready", "tap", "pad_zero", "rope_ready", "sin_in", "sin_out", "q_raw", "q_ss",
            "q_rc", "q_rt", "q_normed", "q_rot", "q_done", "v_ev", "scores2_ps", "logits2_out", "logits2_ready",
            "exp2_ready", "probs2_ready", "transposed2_ps", "pt2_ready", "o2_ps", "o2_ev", "ln_ps", "ln_mid", "ln_sq",
            "ln_rc", "ln_rt", "ln_mul", "ln_out", "wq_ev", "sub_ps", "sub_ev", "experts_in", "soft_in", "soft_ex",
            "route_ready", "et_ps", "et_ev", "onehot_ready", "gates_ps", "gates_used", "seed_ps", "y_ready",
            "y_last"))

        w_ready = [sem(f"w_ready{s}") for s in range(RING)]
        w_used = sem("w_used")
        z_pad = sem("z_pad")
        s_x, s_par, s_con, s_con2, s_tab, s_lr, s_dist, s_dist2 = (sem(n) for n in (
            "x_in", "par_in", "con_in", "con2_in", "tab_in", "lowrank_in", "dist_out", "dist_back"))
        sq_ready, ss_ready, rs_ready, rstd_ready, u_ready, res_ready = (sem(n) for n in (
            "sq_ready", "ss_ready", "rs_ready", "rstd_ready", "u_ready", "res_ready"))
        dve_own, act_own, pool_own = sem("dve_own"), sem("act_own"), sem("pool_own")
        qkv_ev, z_raw, z_ready, low_ready = sem("qkv_ev"), sem("z_raw"), sem("z_ready"), sem("low_ready")
        dist_ps, dist_sb = sem("dist_ps"), sem("dist_sb")
        bc_in, bc_used = [sem("bc_in0"), sem("bc_in1")], sem("bc_used")
        sc_ps, lg_ready, ex_ready, pn_ready, tp_ps, pt_ready, o_ps, o_ev = (sem(n) for n in (
            "scores_ps", "logits_ready", "exp_ready", "probs_ready", "transposed_ps", "pt_ready", "o_ps", "o_ev"))
        lr_ps, lr_act, g_ev, kk_sq, ss_kk, kk_rc, kk_rt, bo_in, bo_ps, bo_used, lc_ready, e_ready = (
            sem(n) for n in ("lowrank_ps", "lowrank_act", "g_ev", "kk_sq", "kk_ss", "kk_rc", "kk_rt", "bonus_in",
                             "bonus_ps", "bonus_used", "logdecay_ready", "exps_ready"))
        c_ps, c_tr, c_dve, c_act, i_ps, i_act, i_dve, r_ps, r_ev, v_ps, y_ps, n_ps, uv_ev, st_ev, y_ev = (
            sem(n) for n in ("c_ps", "c_tr", "c_dve", "c_act", "inv_ps", "inv_act", "inv_dve", "rhs_ps", "rhs_ev",
                             "u_ps", "y_ps", "state_ps", "u_ev", "state_ev", "y_ev"))
        gu_ev, gs_ready, gn_in, gn_mu, gn_sq, gn_var, gn_rc, gn_rt, gn_out = (sem(n) for n in (
            "gu_ev", "silu_ready", "gn_in", "gn_mu", "gn_sq", "gn_var", "gn_rc", "gn_rt", "gn_out"))

        block = ctx.enter_context(nc.Block())

        @block.sync
        def _(sp):
            def stream(name, dram, width=SLOT):
                n, base = dram.shape[0], BASE[name]

                def one(g, j):
                    slot = (base + j) % RING
                    sp.dma_start(ring[:, slot, 0:width], dram[bass.ds(g, 1)].rearrange("a p n -> p (a n)"))\
                        .then_inc(w_ready[slot], 16)

                head = RING if base == 0 else 0
                for j in range(head):
                    one(j, j)
                turns = n // RING
                with sp.Fori(head // RING, turns) as i:
                    for j in range(RING):
                        sp.wait_ge(w_used, i * RING + (base + j - RING + 1))
                        one(i * RING + j, j)
                for j in range(turns * RING, n):
                    sp.wait_ge(w_used, base + j - RING + 1)
                    one(j, j)

            stream("qkv", A["w_qkv"])
            stream("z", A["w_z"])
            stream("out", A["w_out"])
            stream("gu", A["w_gu"])
            stream("down", A["w_down"], DOWN_KT * P)
            stream("in2", A["w_in2"])
            stream("out2", A["w_out2"])
            stream("wq", A["w_wq"])
            stream("u", A["w_u"])
            stream("v", A["w_v"].rearrange("i j d -> j i d"))
            for c in range(DT // 4):
                sp.wait_ge(y_ready, c + 1)
                sp.dma_start(A["y"].rearrange("(c p) t -> p c t", p=P)[:, 4 * c:4 * c + 4, :],
                             xT[:, 4 * c:4 * c + 4, :]).then_inc(s_y, 16)
            sp.wait_ge(s_y, 64)


        @block.gpsimd
        def _(pool):
            pool.wait_ge(dist_sb, 1)
            pool.dma_start(dist_dram, misc[0:NH, 1024:1408].unsqueeze(1).to_broadcast([NH, P, 384])).then_inc(s_dist, 16)
            pool.wait_ge(s_dist, 16)
            for h in range(NH):
                if h >= 2:
                    pool.wait_ge(bc_used, h - 1)
                row = dist_dram[h, 0:1, 127:128]
                two = bass.AP(tensor=row.tensor, offset=row.offset, ap=[[383, P], [1, 256]])
                one = bass.AP(tensor=row.tensor, offset=row.offset + 128, ap=[[383, P], [1, 128]])
                pool.dma_start(BC[:, h % 2, 0:256], two).then_inc(bc_in[h % 2], 16)
                pool.dma_start(BC[:, h % 2, 256:384], one).then_inc(bc_in[h % 2], 16)
            pool.wait_ge(w_used, BASE["gu"])
            pool.dma_start(KEYS, A["keys"]).then_inc(s_keys, 16)
            pool.dma_start(ropt[:, 0, :].bitcast(I32), A["pos"].to_broadcast([P, T])).then_inc(s_pos, 16)
            pool.dma_start(sinkr, A["sinks"].to_broadcast([P, NH])).then_inc(s_sink, 16)
            pool.dma_start(bvr[0:1, :], A["b_v"]).then_inc(s_bv, 16)


        @block.tensor
        def _(pe):
            def arrived(g):
                pe.wait_ge(w_ready[g % RING], 16 * (g // RING + 1))

            def accumulate(out, slot, rhs, kt=DT, first=True, last=True):
                for c in range(kt):
                    ins = pe.matmul(out, ring[:, slot, c * P:(c + 1) * P], rhs(c),
                                    start=first and c == 0, stop=last and c == kt - 1)
                return ins

            def norm_sum(m):
                for c in range(DT):
                    pe.wait_ge(sq_ready, DT * m + c + 1)
                    ins = pe.matmul(bank(2)[:, 0:T], ones, uT[:, c, :], start=c == 0, stop=c == DT - 1)
                ins.then_inc(ss_ready, 1)
                pe.wait_ge(u_ready, DT * (m + 1))

            def loop(name, turns, at, evac, before, rhs):
                g0 = BASE[name] + at
                with pe.Fori(0, turns) as i:
                    for j in range(RING):
                        slot = (g0 + j) % RING
                        pe.wait_ge(w_ready[slot], i * 16 + 16 * ((g0 + j) // RING + 1))
                        pe.wait_ge(evac, i * RING + (before + at + j - 1))
                        accumulate(bank((at + j) % 2)[:, 0:T], slot, rhs).then_inc(w_used, 1)

            u = lambda c: uT[:, c, :]
            mix = lambda c: mixT[:, c, :]
            pe.wait_ge(s_con, 16)
            pe.wait_ge(s_tab, 32)
            pe.matmul(bank(3)[0:NH, 0:384], misc[0:32, 512:528], misc[0:32, 640:1024], start=True, stop=True)\
                .then_inc(dist_ps, 1)
            norm_sum(0)
            for j in range(RING):
                arrived(j)
                if j >= 2:
                    pe.wait_ge(qkv_ev, j - 1)
                accumulate(bank(j % 2)[:, 0:T], j, u).then_inc(w_used, 1)
            loop("qkv", 3, 4, qkv_ev, 0, u)
            with pe.Fori(0, 2) as i:
                for j in range(RING):
                    pe.wait_ge(w_ready[j], i * 16 + 16 * 5)
                    pe.wait_ge(qkv_ev, i * RING + (16 + j - 1))
                    for t in range(2):
                        for c in range(DT):
                            ins = pe.matmul(bank(j % 2)[:, t * P:(t + 1) * P], uT[:, c, t * P:(t + 1) * P],
                                            ring[:, j, c * P:(c + 1) * P], start=c == 0, stop=c == DT - 1)
                    ins.then_inc(w_used, 1)

            def scores(h, q, k, done):
                hp = HD * (h % 2)
                out = bank(2)
                pe.matmul(out[:, 0:256], q[hp:hp + HD, P:T], k[hp:hp + HD, :], start=True, stop=True)
                pe.matmul(out[:, 256:384], q[hp:hp + HD, 0:P], k[hp:hp + HD, 0:P], start=True, stop=True)\
                    .then_inc(done, 1)

            def turn_probs(h, probs, done):
                for b in range(3):
                    ins = pe.transpose(bank(3)[:, b * P:(b + 1) * P], probs[:, b * P:(b + 1) * P], ident)
                ins.then_inc(done, 1)

            def weigh_v(h, v, pt, done):
                hp = HD * (h % 2)
                out = bank(4)[hp:hp + HD, 0:T]
                pe.matmul(out[:, P:T], v(0), pt[:, 0:P], start=True, stop=False)
                pe.matmul(out[:, P:T], v(1), pt[:, P:2 * P], start=False, stop=True)
                pe.matmul(out[:, 0:P], v(0), pt[:, 2 * P:3 * P], start=True, stop=True).then_inc(done, 1)

            def lowrank(i):
                col = slice(i * P, (i + 1) * P)
                if i == 0:
                    pe.wait_ge(low_ready, 3)
                    pe.wait_ge(s_lr, 64)
                else:
                    pe.wait_ge(lr_act, 2 * i)
                    pe.wait_ge(g_ev, i)
                pe.matmul(bank(6)[:, 0:T], LR[0:64, 0, col], lo[0:64, 0, :], start=True, stop=True)
                pe.matmul(bank(7)[:, 0:T], LR[:, 1, col], lo[:, 1, :], start=True, stop=False)
                pe.matmul(bank(7)[:, 0:T], LR2[0:32, col], lo[0:32, 2, :], start=False, stop=True)
                pe.matmul(bank(7)[:, T:2 * T], LR[64:128, 0, col], lo[64:128, 0, :], start=True, stop=True)\
                    .then_inc(lr_ps, 1)

            def head_sums(i):
                pe.wait_ge(kk_sq, i + 1)
                if i:
                    pe.wait_ge(bo_used, i)
                pe.matmul(bank(5)[:, 0:T], blk, sc[:, 5, :], start=True, stop=True).then_inc(ss_kk, 1)
                pe.wait_ge(bo_in, i + 1)
                pe.wait_ge(kk_rc, i + 1)
                pe.matmul(bank(5)[:, 0:T], blk, sc[:, 6, :], start=True, stop=True).then_inc(bo_ps, 1)

            for c in range(27):
                g = BASE["z"] + c
                arrived(g)
                if c < 2:
                    pe.wait_ge(qkv_ev, 23 + c)
                else:
                    pe.wait_ge(z_raw, c - 1)
                accumulate(bank(c % 2)[:, 0:T], g % RING, u).then_inc(w_used, 1)
                if c < NH:
                    if c == 0:
                        pe.wait_ge(qkv_ev, 24)
                    if c:
                        pe.wait_ge(bc_used, c)
                    scores(c, QK[:, c // 2, :], QK[:, 8 + c // 2, :], sc_ps)
                if 1 <= c <= NH:
                    pe.wait_ge(pn_ready, c)
                    if c >= 2:
                        pe.wait_ge(pt_ready, c - 1)
                    turn_probs(c - 1, LG[:, (c - 1) % 2, :], tp_ps)
                if 2 <= c <= NH + 1:
                    h = c - 2
                    pe.wait_ge(pt_ready, h + 1)
                    if h >= 2 and h % 2 == 0:
                        pe.wait_ge(o_ev, h // 2)
                    weigh_v(h, lambda s, h=h: VN[:, s, h * HD:(h + 1) * HD], PT[:, h % 2, :], o_ps)
                if c >= 3 and c % 3 == 0:
                    lowrank(c // 3 - 1)
                if c >= 5 and c % 3 == 2:
                    head_sums(c // 3 - 1)

            for c in range(NC_):
                if c == 0:
                    pe.wait_ge(bo_used, WT)
                if c:
                    pe.wait_ge(y_ev, c)
                    pe.wait_ge(st_ev, c)
                for i in range(WT):
                    pe.transpose(bank(i // 4)[:, (i % 4) * P:(i % 4 + 1) * P], BK[:, i, c, :], ident)
                for i in range(WT):
                    ins = pe.transpose(bank(2 + i // 4)[0:CH, (i % 4) * P:(i % 4 + 1) * P],
                                       vT[:, i, c * CH:(c + 1) * CH], ident)
                ins.then_inc(c_tr, 1)
                for h in range(NH):
                    hp = HD * (h % 2)
                    k = h // 2
                    ins = pe.matmul(bank(4 + 2 * (h % 2) + k // 4)[:, (k % 4) * P:(k % 4 + 1) * P],
                                    BK[hp:hp + HD, k, c, :], AR[hp:hp + HD, k, c, :], start=True, stop=True)
                ins.then_inc(c_ps, 1)
                pe.wait_ge(c_act, 4 * c + 2)
                for h in range(NH):
                    hp = HD * (h % 2)
                    k = h // 2
                    ins = pe.matmul(bank(0)[hp:hp + HD, k * CH:(k + 1) * CH], AR[hp:hp + HD, k, c, 0:CH],
                                    BK[hp:hp + HD, k, c, 0:CH], start=True, stop=True)
                ins.then_inc(c_ps, 1)
                for n, step in enumerate(INVERSE):
                    if n == 0:
                        pe.wait_ge(c_dve, c + 1)
                        pe.wait_ge(c_act, 4 * c + 4)
                    if EVA[n] + c:
                        pe.wait_ge(i_act, EVA[NSTEP] * c + EVA[n])
                    if EVD[n] + c:
                        pe.wait_ge(i_dve, EVD[NSTEP] * c + EVD[n])
                    for a, b, at, _ in step:
                        for h in range(NH):
                            hp, k = HD * (h % 2), h // 2
                            rhs = cst("i64")[hp:hp + HD, :] if b == "i" else Bf[b][hp:hp + HD, k, :]
                            ins = pe.matmul(bank(at)[hp:hp + HD, k * CH:(k + 1) * CH],
                                            Bf[a][hp:hp + HD, k, :], rhs, start=True, stop=True)
                    ins.then_inc(i_ps, 1)
                pe.wait_ge(i_dve, EVD[NSTEP] * (c + 1))
                pe.wait_ge(i_act, EVA[NSTEP] * (c + 1))
                for h in range(NH):
                    hp, k = HD * (h % 2), h // 2
                    ins = pe.matmul(bank(0)[hp:hp + HD, k * CH:(k + 1) * CH], QS[:, h, 0:CH], SV[:, h, :],
                                    start=True, stop=True)
                ins.then_inc(r_ps, 1)
                pe.wait_ge(r_ev, c + 1)
                for h in range(NH):
                    hp, k = HD * (h % 2), h // 2
                    ins = pe.matmul(bank(4 + h % 2)[0:CH, k * CH:(k + 1) * CH], Bf[8][hp:hp + HD, k, :],
                                    Bf[3][hp:hp + HD, k, :], start=True, stop=True)
                ins.then_inc(v_ps, 1)
                pe.wait_ge(uv_ev, c + 1)
                for h in range(NH):
                    hp, k = HD * (h % 2), h // 2
                    out = bank(6)[hp:hp + HD, k * CH:(k + 1) * CH]
                    pe.matmul(out, SV[:, h, :], QS[:, h, CH:P], start=True, stop=False)
                    ins = pe.matmul(out, UV[0:CH, h, :], MB[0:CH, h, CH:P], start=False, stop=True)
                ins.then_inc(y_ps, 1)
                for h in range(NH) if c < NC_ - 1 else ():
                    ins = pe.matmul(bank(2 + h // 8)[0:CH, (h % 8) * CH:(h % 8 + 1) * CH], BKn[:, h, :],
                                    UV[:, h, :], start=True, stop=True)
                if c < NC_ - 1:
                    ins.then_inc(n_ps, 1)

            for i in range(WT):
                if i == 0:
                    pe.wait_ge(y_ev, NC_)
                if i >= 2:
                    pe.wait_ge(gn_in, i - 1)
                pe.matmul(bank(i % 2)[:, 0:T], blk, yv[:, i, :, :], start=True, stop=True).then_inc(gn_mu, 1)
                if i:
                    pe.wait_ge(gn_sq, i)
                    if i >= 3:
                        pe.wait_ge(gn_rc, i - 2)
                    pe.matmul(bank(4 + (i - 1) % 2)[:, 0:T], blk, sc[:, (i - 1) % 2, :], start=True, stop=True)\
                        .then_inc(gn_var, 1)
            pe.wait_ge(gn_sq, WT)
            pe.matmul(bank(5)[:, 0:T], blk, sc[:, 1, :], start=True, stop=True).then_inc(gn_var, 1)

            pe.wait_ge(o_ev, WT)
            pe.wait_ge(gn_out, WT)
            for c in range(DT):
                g = BASE["out"] + c
                arrived(g)
                if c >= 2:
                    pe.wait_ge(res_ready, c - 1)
                accumulate(bank(c % 2)[:, 0:T], g % RING, mix).then_inc(w_used, 1)
            norm_sum(1)
            g0 = BASE["gu"]

            def gate_up(i, first):
                for j in range(RING):
                    slot = (g0 + j) % RING
                    pe.wait_ge(w_ready[slot], i * 16 + 16 * ((g0 + j) // RING + 1))
                    if not first:
                        pe.wait_ge(gu_ev, i * 2 + (j // 2 - 1))
                    accumulate(bank(j)[:, 0:T], slot, u).then_inc(w_used, 1)

            gate_up(0, True)
            with pe.Fori(1, FT // 2) as i:
                gate_up(i, False)
            g0d = BASE["down"]
            pe.wait_ge(gu_ev, FT)

            def down(i, first):
                for t in range(2):
                    if not first:
                        pe.wait_ge(res_ready, i * 2 + (DT + t - 1))
                    for q in range(RING):
                        slot = (g0d + 4 * t + q) % RING
                        pe.wait_ge(w_ready[slot], i * 32 + 16 * ((g0d + 4 * t + q) // RING + 1))
                        accumulate(bank(t)[:, 0:T], slot, lambda c: GT[:, DOWN_KT * q + c, :], DOWN_KT,
                                   q == 0, q == RING - 1).then_inc(w_used, 1)

            down(0, True)
            with pe.Fori(1, DT // 2) as i:
                down(i, False)
            norm_sum(2)
            norm_sum(3)
            g0 = BASE["in2"]

            def conv_inputs(i, first):
                for j in range(RING):
                    slot = (g0 + j) % RING
                    pe.wait_ge(w_ready[slot], i * 16 + 16 * ((g0 + j) // RING + 1))
                    if not first:
                        pe.wait_ge(cv_ev, i * 2 + (j // 2 - 1))
                    accumulate(bank(j)[:, 0:T], slot, u).then_inc(w_used, 1)

            conv_inputs(0, True)
            with pe.Fori(1, CONV_TILES // RING) as i:
                conv_inputs(i, False)
            pe.wait_ge(cv_ev, WT)
            for n in range(12):
                if n < 10:
                    arrived(Q0 + n)
                    if n >= 2:
                        pe.wait_ge(q_raw, n - 1)
                    slot = (Q0 + n) % RING
                if n < 9:
                    accumulate(bank(n % 2)[:, 0:T], slot, u).then_inc(w_used, 1)
                if n == 9:
                    pe.wait_ge(s_bv, 16)
                    for t in range(2):
                        for c in range(DT):
                            pe.matmul(bank(1)[:, t * P:(t + 1) * P], uT[:, c, t * P:(t + 1) * P],
                                      ring[:, slot, c * P:(c + 1) * P], start=c == 0, stop=False)
                        ins = pe.matmul(bank(1)[:, t * P:(t + 1) * P], ones[0:1, :], bvr[0:1, :],
                                        start=False, stop=True)
                    ins.then_inc(w_used, 1)
                if 1 <= n <= 9:
                    m = n - 1
                    pe.wait_ge(q_raw, m + 1)
                    if m:
                        pe.wait_ge(q_rc, m)
                    pe.matmul(bank(4)[:, 0:T], blk, qsq[:, m % 2, :], start=True, stop=True).then_inc(q_ss, 1)
                if 2 <= n <= 10:
                    m = n - 2
                    pe.wait_ge(q_nm, m + 1)
                    if m:
                        pe.wait_ge(q_done, m)
                    pe.matmul(bank(5)[:, 0:T], cst("perm"), qnm[:, m % 2, :], start=True, stop=True).then_inc(q_rot, 1)
            for c in range(WT):
                if c == 0:
                    pe.wait_ge(tap, WT * CONV_K)
                ins = pe.matmul(bank(6)[:, 0:T], ones, mix2[:, c, :], start=c == 0, stop=c == WT - 1)
            ins.then_inc(ln_ps, 1)
            for c in range(WT):
                pe.wait_ge(ln_sq, c + 1)
                ins = pe.matmul(bank(7)[:, 0:T], ones, HS[:, c, :], start=c == 0, stop=c == WT - 1)
            ins.then_inc(ln_ps, 1)
            pe.wait_ge(q_done, 9)
            pe.wait_ge(v_ev, 1)
            for c in range(NH + 2):
                if c < NH:
                    if c:
                        pe.wait_ge(lg2_used, c)
                    scores(c, QR[:, c // 2, :], KR, sc2_ps)
                if 1 <= c <= NH:
                    pe.wait_ge(pn2_ready, c)
                    if c >= 2:
                        pe.wait_ge(pt2_ready, c - 1)
                    turn_probs(c - 1, LG2[:, (c - 1) % 2, :], tp2_ps)
                if c >= 2:
                    h = c - 2
                    e = h % 2
                    pe.wait_ge(pt2_ready, h + 1)
                    if h >= 2 and e == 0:
                        pe.wait_ge(o2_ev, h // 2)
                    weigh_v(h, lambda s: VB[:, s, HD * e:HD * e + HD], PT2[:, e, :], o2_ps)
            pe.wait_ge(ln_out, WT)
            pe.wait_ge(o2_ev, WT)
            for c in range(DT):
                g = BASE["out2"] + c
                arrived(g)
                if c >= 2:
                    pe.wait_ge(res_ready, 2 * DT + c - 1)
                accumulate(bank(c % 2)[:, 0:T], g % RING, lambda c: mix2[:, c, :]).then_inc(w_used, 1)
            norm_sum(4)
            for j in range(RING):
                g = BASE["wq"] + j
                arrived(g)
                if j >= 2:
                    pe.wait_ge(wq_ev, j - 1)
                accumulate(bank(j % 2)[:, 0:T], g % RING, u).then_inc(w_used, 1)
            loop("wq", 3, 4, wq_ev, 0, u)
            pe.wait_ge(wq_ev, DT)
            pe.wait_ge(s_keys, 16)
            for t in range(2):
                for n in range(2 * PH):
                    ins = pe.matmul(bank(4 * (1 - t) + n // 4)[:, (n % 4) * P:(n % 4 + 1) * P],
                                    HQ[:, n, t * P:(t + 1) * P], KEYS[:, n * NK:(n + 1) * NK], start=True, stop=True)
                ins.then_inc(sub_ps, 1)

            def experts_in(i, first):
                for j in range(RING):
                    g = BASE["u"] + j
                    pe.wait_ge(w_ready[g % RING], i * 16 + 16 * (g // RING + 1))
                    if not first:
                        pe.wait_ge(u_ev, i * RING + (j - RING + 1))
                    accumulate(bank(j)[:, 0:T], g % RING, u).then_inc(w_used, 1)

            pe.wait_ge(sub_ev, 8)
            experts_in(0, True)
            with pe.Fori(1, 16) as i:
                experts_in(i, False)
            pe.wait_ge(route_ready, 2)
            for t in range(2):
                for n in range(3):
                    ins = pe.transpose(bank(4 + t)[:, n * P:(n + 1) * P], exs[:, t, n, :], ident)
            ins.then_inc(et_ps, 1)
            with pe.Fori(16, 32) as i:
                experts_in(i, False)
            pe.wait_ge(u_ev, NK)

            def gates(i, b, first):
                pe.wait_ge(oh_ready, i * 2 + (b + 1))
                if not first:
                    pe.wait_ge(g_used, i * 2 + (b - 1))
                for t in range(4):
                    ins = pe.matmul(bank(4 + b)[:, t * P:(t + 1) * P], OH[:, b, 0, t, :], OH[:, b, 1, t, :],
                                    start=True, stop=True)
                ins.then_inc(g_ps, 1)

            for b in range(2):
                gates(0, b, True)
            with pe.Fori(1, 32) as i:
                for b in range(2):
                    gates(i, b, False)
            pe.wait_ge(g_used, 64)
            for d in range(DT):
                pe.matmul(bank(d // 2)[:, (d % 2) * T:(d % 2 + 1) * T], ident, xT[:, d, :], start=d % 2 == 0,
                          stop=False, skip_group_check=True)
            with pe.Fori(0, NK // RING) as i:
                for j in range(RING):
                    g = BASE["v"] + j
                    pe.wait_ge(w_ready[g % RING], i * 16 + 16 * (g // RING + 1))
                    for d in range(DT):
                        ins = pe.matmul(bank(d // 2)[:, (d % 2) * T:(d % 2 + 1) * T],
                                        ring[:, g % RING, d * P:(d + 1) * P],
                                        HB[:, bass.ds(i * RING + j, 1), :].rearrange("p a t -> p (a t)"),
                                        start=False, stop=False, skip_group_check=True)
                    ins.then_inc(w_used, 1)


        @block.scalar
        def _(act):
            act.dma_start(par[:, :], A["par"]).then_inc(s_par, 16)
            act.dma_start(con[:, :], A["con"][:, 0:KEEP]).then_inc(s_con, 16)
            act.dma_start(xT[:, :, :], A["x"].rearrange("(c p) t -> p c t", p=P)).then_inc(s_x, 16)
            act.dma_start(misc[0:32, 512:528], A["table"]).then_inc(s_tab, 16)
            act.dma_start(misc[0:48, 640:1024], A["dist"]).then_inc(s_tab, 16)
            act.dma_start(arena[:, 0:TAIL], A["con"][:, KEEP:NCON]).then_inc(s_con2, 16)
            act.dma_start(LR[0:64, 0, :], A["w_up"]).then_inc(s_lr, 16)
            act.dma_start(LR[64:128, 0, :], A["a_up"]).then_inc(s_lr, 16)
            act.dma_start(LR[:, 1, :], A["g_up"][0:P, :]).then_inc(s_lr, 16)
            act.dma_start(LR2[0:32, :], A["g_up"][P:P + 32, :]).then_inc(s_lr, 16)

            def squares(m, ready, before):
                for c in range(DT):
                    act.wait_ge(ready, before + (c + 1 if ready is not s_x else 0))
                    act.activation(uT[:, c, :], xT[:, c, :], ACT.Square).then_inc(sq_ready, 1)
                act.wait_ge(rs_ready, m + 1)
                act.activation(rstd, nrm, ACT.Sqrt).then_inc(rstd_ready, 1)

            squares(0, s_x, 16)
            with act.Fori(0, 4) as i:
                for j in range(RING):
                    act.wait_ge(w_used, i * RING + (j + 1))
                    act.activation(QK[:, bass.ds(i * RING + j, 1), :], ps[:, j % 2:j % 2 + 1, 0:T], ACT.Copy)\
                        .then_inc(qkv_ev, 1)
            with act.Fori(0, 2) as i:
                for j in range(RING):
                    act.wait_ge(w_used, i * RING + (16 + j + 1))
                    act.activation(VN[:, :, bass.ds((i * RING + j) * P, P)],
                                   bank(j % 2)[:, 0:T].rearrange("p (s n) -> p s n", s=2), ACT.Copy)\
                        .then_inc(qkv_ev, 1)

            def exps(h, logits, ready, used):
                act.wait_ge(ready, h + 1)
                s4 = small[:, 8 * (h % 2):8 * (h % 2) + 8]
                act.activation(logits[:, 0:256], logits[:, 0:256], ACT.Exp, bias=s4[:, 2:3],
                               accum_out=s4[:, 4:5])
                act.activation(logits[:, 256:384], logits[:, 256:384], ACT.Exp, bias=s4[:, 3:4],
                               accum_out=s4[:, 5:6]).then_inc(used, 1)

            for c in range(27):
                act.wait_ge(w_used, BASE["z"] + c + 1)
                if c >= 2:
                    act.wait_ge(z_ready, c - 1)
                else:
                    act.wait_ge(z_pad, 1)
                act.activation(zraw[:, c % 2, 1:T + 1], bank(c % 2)[:, 0:T], ACT.Copy).then_inc(z_raw, 1)
                if c < NH:
                    exps(c, LG[:, c % 2, :], lg_ready, ex_ready)
                if c == 3:
                    act.wait_ge(z_ready, 3)
                    act.activation(lo[0:64, 0, :], lo[0:64, 0, :], ACT.Tanh).then_inc(low_ready, 1)
                    act.activation(lo[:, 1, :], lo[:, 1, :], ACT.Sigmoid).then_inc(low_ready, 1)
                    act.activation(lo[0:32, 2, :], lo[0:32, 2, :], ACT.Sigmoid).then_inc(low_ready, 1)
                if c >= 3 and c % 3 == 0:
                    i = c // 3 - 1
                    act.wait_ge(lr_ps, i + 1)
                    if i:
                        act.wait_ge(bo_used, i)
                    act.activation(sc[:, 2, :], bank(6)[:, 0:T], ACT.Sigmoid, bias=prm("w0", i)).then_inc(lr_act, 1)
                    act.activation(sc[:, 3, :], bank(7)[:, T:2 * T], ACT.Sigmoid, bias=prm("a0", i))\
                        .then_inc(lr_act, 1)
                    act.activation(gT[:, i, :], bank(7)[:, 0:T], ACT.Copy).then_inc(g_ev, 1)
                if c >= 5 and c % 3 == 2:
                    i = c // 3 - 1
                    act.wait_ge(lc_ready, i + 1)
                    cut = lambda s: sc[:, s, :].rearrange("p (n t) -> p n t", n=NC_)
                    act.activation(AR[:, i, :, CH:P], cut(7), ACT.Exp)
                    act.activation(BK[:, i, :, CH:P], cut(7), ACT.Exp, scale=-1.0)
                    act.activation(AR[:, i, :, 0:CH], cut(8), ACT.Exp).then_inc(e_ready, 1)
                    act.wait_ge(kk_rc, i + 1)
                    act.activation(sc[:, 9, :], sc[:, 11, :], ACT.Sqrt).then_inc(kk_rt, 1)
                if 1 <= c <= NH:
                    h = c - 1
                    act.wait_ge(tp_ps, h + 1)
                    if h >= 2:
                        act.wait_ge(o_ps, h - 1)
                    act.activation(PT[:, h % 2, :], bank(3)[:, 0:384], ACT.Copy).then_inc(pt_ready, 1)
                if 2 <= c <= NH + 1 and c % 2 == 1:
                    act.wait_ge(o_ps, c - 1)
                    act.activation(mixT[:, (c - 3) // 2, :], bank(4)[:, 0:T], ACT.Copy).then_inc(o_ev, 1)

            AR4 = AR[:, :, :, :]
            QS4 = QS.rearrange("p (k e) n -> p e k n", e=2)
            for c in range(NC_):
                act.wait_ge(c_tr, c + 1)
                for b in range(2):
                    act.activation(BKn[:, 8 * b:8 * b + 8, :], bank(b).rearrange("p (h n) -> p h n", h=8), ACT.Copy)\
                        .then_inc(c_act, 1)
                for e in range(2):
                    act.activation(QS4[0:CH, e, :, :], AR4[HD * e:HD * e + HD, :, c, :], ACT.Copy)\
                        .then_inc(c_act, 1)
                for n, step in enumerate(INVERSE):
                    act.wait_ge(i_ps, NSTEP * c + n + 1)
                    for _, _, at, evs in step:
                        for engine, to in evs:
                            if engine == "act":
                                act.activation(Bf[to], bank(at).rearrange("p (k n) -> p k n", k=8), ACT.Copy)\
                                    .then_inc(i_act, 1)
                act.wait_ge(r_ps, c + 1)
                act.activation(Bf[3], bank(0).rearrange("p (k n) -> p k n", k=8), ACT.Copy).then_inc(r_ev, 1)
                act.wait_ge(y_ps, c + 1)
                act.activation(yv[:, :, c, :], bank(6).rearrange("p (k n) -> p k n", k=8), ACT.Copy)\
                    .then_inc(y_ev, 1)

            for i in range(WT):
                act.wait_ge(gn_in, i + 1)
                if i >= 2:
                    act.wait_ge(gn_var, i - 1)
                act.activation(sc[:, i % 2, :].rearrange("p (n t) -> p n t", n=NC_), yv[:, i, :, :], ACT.Square)\
                    .then_inc(gn_sq, 1)
                act.wait_ge(gn_rc, i + 1)
                act.activation(sc[:, 4 + i % 2, :], sc[:, 2 + i % 2, :], ACT.Sqrt).then_inc(gn_rt, 1)

            squares(1, res_ready, 0)
            with act.Fori(0, FT // 2) as i:
                for j in range(2):
                    act.wait_ge(w_used, i * RING + (BASE["gu"] + 2 * j + 1))
                    act.activation(GS[:, j, :], bank(2 * j)[:, 0:T], ACT.Silu).then_inc(gs_ready, 1)
            squares(2, res_ready, DT)
            squares(3, u_ready, 3 * DT - DT)
            act.wait_ge(sin_in, 1)
            act.activation(sinT, ropt[:, 1, :], ACT.Sin)
            act.activation(cosT, posf, ACT.Sin).then_inc(sin_out, 1)
            with act.Fori(0, WT // 2) as i:
                for j in range(2):
                    act.wait_ge(w_used, i * RING + (BASE["in2"] + 2 * j + 2))
                    act.activation(sg[:, j, :], bank(2 * j + 1)[:, 0:T], ACT.Sigmoid,
                                   bias=par[:, bass.ds(i * RING + (PAR["bin2"][0] + 2 * j + 1), 1)])\
                        .then_inc(sg_ready, 1)
            for n in range(10):
                if n < 9:
                    act.wait_ge(w_used, Q0 + n + 1)
                    if n >= 2:
                        act.wait_ge(q_nm, n - 1)
                    act.activation(qraw[:, n % 2, :], bank(n % 2)[:, 0:T], ACT.Identity, bias=prm("bin2", 16 + n))\
                        .then_inc(act_own, 1)
                    act.wait_ge(act_own, n + 1)
                    act.activation(qsq[:, n % 2, :], qraw[:, n % 2, :], ACT.Square).then_inc(q_raw, 1)
                if n >= 1:
                    act.wait_ge(q_rc, n)
                    act.activation(qsc[:, 1, :], qsc[:, 0, :], ACT.Sqrt).then_inc(q_rt, 1)
            act.wait_ge(w_used, Q0 + 10)
            act.activation(VB, bank(1)[:, 0:T].rearrange("p (s n) -> p s n", s=2), ACT.Copy).then_inc(v_ev, 1)
            act.wait_ge(ln_mid, 1)
            for c in range(WT):
                act.activation(HS[:, c, :], mix2[:, c, :], ACT.Square).then_inc(ln_sq, 1)
            act.wait_ge(ln_rc, 1)
            act.activation(rstd, nrm, ACT.Sqrt).then_inc(ln_rt, 1)
            act.wait_ge(ln_mul, 1)
            for c in range(WT):
                act.activation(mix2[:, c, :], mix2[:, c, :], ACT.Silu, bias=prm("clb", c), scale=prm("clg", c))\
                    .then_inc(ln_out, 1)
            for c in range(NH + 2):
                if c < NH:
                    act.wait_ge(lg2_ready, c + 1)
                    s4 = small[:, 16 * (c % 2):16 * (c % 2) + 16]
                    act.activation(s4[:, 8:10], s4[:, 2:4], ACT.Exp, bias=sinkr[:, c:c + 1])
                    act.activation(LG2[:, c % 2, 0:256], LG2[:, c % 2, 0:256], ACT.Exp, bias=s4[:, 2:3],
                                   accum_out=s4[:, 4:5])
                    act.activation(LG2[:, c % 2, 256:384], LG2[:, c % 2, 256:384], ACT.Exp, bias=s4[:, 3:4],
                                   accum_out=s4[:, 5:6]).then_inc(ex2_ready, 1)
                if 1 <= c <= NH:
                    h = c - 1
                    act.wait_ge(tp2_ps, h + 1)
                    if h >= 2:
                        act.wait_ge(o2_ps, h - 1)
                    act.activation(PT2[:, h % 2, :], bank(3)[:, 0:384], ACT.Copy).then_inc(pt2_ready, 1)
                if c >= 2 and c % 2 == 1:
                    act.wait_ge(o2_ps, c - 1)
                    act.activation(mix2[:, WT + (c - 3) // 2, :], bank(4)[:, 0:T], ACT.Copy).then_inc(o2_ev, 1)
            squares(4, res_ready, 2 * DT)
            with act.Fori(0, 4) as i:
                for j in range(RING):
                    act.wait_ge(w_used, i * RING + (BASE["wq"] + j + 1))
                    act.activation(HQ[:, bass.ds(i * RING + j, 1), :], ps[:, j % 2:j % 2 + 1, 0:T], ACT.Copy)\
                        .then_inc(wq_ev, 1)
            for t in range(2):
                act.wait_ge(sub_ps, t + 1)
                for b in range(4):
                    act.activation(SUB[:, t, 4 * b:4 * b + 4, :],
                                   bank(4 * (1 - t) + b).rearrange("p (n k) -> p n k", n=4), ACT.Copy)\
                        .then_inc(sub_ev, 1)

            def gelus(a, b):
                with act.Fori(a, b) as i:
                    for j in range(RING):
                        act.wait_ge(w_used, i * RING + (BASE["u"] + j + 1))
                        act.activation(HB[:, bass.ds(i * RING + j, 1), :], ps[:, j:j + 1, 0:T], ACT.Gelu)\
                            .then_inc(u_ev, 1)

            gelus(0, 12)
            act.wait_ge(soft_in, 2)
            for t in range(2):
                act.activation(val[:, t, :, :], val[:, t, :, :], ACT.Exp).then_inc(soft_ex, 1)
            gelus(12, 16)
            act.wait_ge(et_ev, 1)
            gelus(16, 32)


        @block.vector
        def _(dve):
            own = [0]

            def link(ins):
                own[0] += 1
                ins.then_inc(dve_own, 1)
                dve.wait_ge(dve_own, own[0])

            def bc(ap, *shape):
                return ap.unsqueeze(1).to_broadcast(list(shape))

            def scale(m, gain, dst):
                dve.wait_ge(ss_ready, m + 1)
                link(dve.tensor_scalar(nrm, bank(2)[:, 0:T], 1.0 / D, RMS_EPS, ALU.mult, ALU.add))
                dve.reciprocal(nrm, nrm).then_inc(rs_ready, 1)
                dve.wait_ge(rstd_ready, m + 1)
                for c in range(DT):
                    dve.scalar_tensor_tensor(out=dst[:, c, :], in0=xT[:, c, :], scalar=prm(gain, c), in1=rstd,
                                             op0=ALU.mult, op1=ALU.mult).then_inc(u_ready, 1)

            dve.memset(zraw[:, :, 0:1], 0.0).then_inc(z_pad, 1)
            dve.wait_ge(s_tab, 32)
            dve.wait_ge(dist_ps, 1)
            link(dve.tensor_copy(misc[0:NH, 2560:2944], misc[32:48, 640:1024]))
            dve.tensor_tensor(misc[0:NH, 1024:1408], bank(3)[0:NH, 0:384], misc[0:NH, 2560:2944], ALU.add)\
                .then_inc(dist_sb, 1)
            dve.wait_ge(s_par, 16)
            dve.wait_ge(s_x, 16)
            scale(0, "n1", uT)

            def row_max(h, logits, ready):
                s4 = small[:, 8 * (h % 2):8 * (h % 2) + 8]
                dve.tensor_reduce(s4[:, 0:1], logits[:, 0:256], AX, ALU.max)
                link(dve.tensor_reduce(s4[:, 1:2], logits[:, 256:384], AX, ALU.max))
                dve.tensor_scalar(s4[:, 2:4], s4[:, 0:2], -1.0, None, ALU.mult).then_inc(ready, 1)

            def divide(h, probs, ready):
                s4 = small[:, 8 * (h % 2):8 * (h % 2) + 8]
                link(dve.reciprocal(s4[:, 6:8], s4[:, 4:6]))
                dve.tensor_scalar(probs[:, 0:256], probs[:, 0:256], s4[:, 6:7], None, ALU.mult)
                dve.tensor_scalar(probs[:, 256:384], probs[:, 256:384], s4[:, 7:8], None, ALU.mult)\
                    .then_inc(ready, 1)

            dve.wait_ge(s_con2, 16)
            for c in range(27):
                if c < NH:
                    h = c
                    dve.wait_ge(sc_ps, h + 1)
                    dve.wait_ge(bc_in[h % 2], 32 * (h // 2 + 1))
                    if h >= 2:
                        dve.wait_ge(tp_ps, h - 1)
                    dve.scalar_tensor_tensor(out=LG[:, h % 2, :], in0=bank(2)[:, 0:384], scalar=HD ** -0.5,
                                             in1=BC[:, h % 2, :], op0=ALU.mult, op1=ALU.add).then_inc(bc_used, 1)
                    dve.wait_ge(bc_used, h + 1)
                    row_max(h, LG[:, h % 2, :], lg_ready)
                dve.wait_ge(z_raw, c + 1)
                if c:
                    dve.wait_ge(z_ready, c)
                z = zraw[:, c % 2, 1:T + 1]
                link(dve.tensor_tensor(zdif, zraw[:, c % 2, 0:T], z, ALU.subtract))
                i = c // 3 - 1
                dst = lo[:, c, :] if c < 3 else (sc[:, 0, :], sc[:, 1, :], vT[:, i, :])[c % 3]
                dve.scalar_tensor_tensor(out=dst, in0=zdif, scalar=prm("mix", c), in1=z, op0=ALU.mult, op1=ALU.add)\
                    .then_inc(z_ready, 1)
                if c < NH:
                    dve.wait_ge(ex_ready, c + 1)
                    divide(c, LG[:, c % 2, :], pn_ready)
                if c < 5 or c % 3 != 2:
                    continue
                dve.wait_ge(z_ready, c + 1)
                dve.wait_ge(lr_act, 2 * i + 2)
                r, k, lw, a, kk, sq, rkk, lc, tmp, t2, kp, rc = (sc[:, n, :] for n in range(12))
                link(dve.tensor_scalar(lw, lw, -DECAY, None, ALU.mult))
                link(dve.tensor_tensor_scan(lc, cst("reset"), lw, 0.0, ALU.mult, ALU.add))
                dve.tensor_tensor(tmp, lc, lw, ALU.subtract).then_inc(lc_ready, 1)
                link(dve.tensor_scalar(kk, k, prm("kk", i), None, ALU.mult))
                dve.tensor_tensor(sq, kk, kk, ALU.mult).then_inc(kk_sq, 1)
                link(dve.tensor_scalar(kp, a, -1.0, prm("ka", i), ALU.add, ALU.mult))
                link(dve.scalar_tensor_tensor(out=kp, in0=kp, scalar=1.0, in1=k, op0=ALU.add, op1=ALU.mult))
                dve.scalar_tensor_tensor(out=rkk, in0=r, scalar=prm("rk", i), in1=kp, op0=ALU.mult, op1=ALU.mult)\
                    .then_inc(bo_in, 1)
                dve.wait_ge(ss_kk, i + 1)
                link(dve.tensor_scalar(rc, bank(5)[:, 0:T], 1e-24, None, ALU.max))
                dve.reciprocal(rc, rc).then_inc(kk_rc, 1)
                dve.wait_ge(kk_rt, i + 1)
                link(dve.tensor_tensor(kk, kk, t2, ALU.mult))
                dve.tensor_tensor(t2, kk, a, ALU.mult)
                dve.wait_ge(e_ready, i + 1)
                cut = lambda s: s.rearrange("p (n t) -> p n t", n=NC_)
                link(dve.tensor_copy(wend[:, i, :].unsqueeze(2), AR[:, i, :, P - 1:P]))
                dve.tensor_tensor(AR[:, i, :, CH:P], AR[:, i, :, CH:P], cut(r), ALU.mult)
                dve.scalar_tensor_tensor(out=AR[:, i, :, 0:CH], in0=AR[:, i, :, 0:CH], scalar=-1.0, in1=cut(kk),
                                         op0=ALU.mult, op1=ALU.mult)
                link(dve.tensor_tensor(BK[:, i, :, 0:CH], BK[:, i, :, CH:P], cut(t2), ALU.mult))
                dve.tensor_tensor(BK[:, i, :, CH:P], BK[:, i, :, CH:P], cut(kp), ALU.mult)
                dve.wait_ge(bo_ps, i + 1)
                dve.tensor_tensor(bonT[:, i, :], bank(5)[:, 0:T], vT[:, i, :], ALU.mult).then_inc(bo_used, 1)

            wend2 = wendh.rearrange("p (k e) n -> p e k n", e=2)
            dve.tensor_copy(wend2[0:HD, 0, :, :], wend[0:HD, :, :])
            link(dve.tensor_copy(wend2[0:HD, 1, :, :], wend[HD:P, :, :]))
            MB4 = MB.rearrange("p (k e) n -> p e k n", e=2)
            QS4 = QS.rearrange("p (k e) n -> p e k n", e=2)
            UV4 = UV.rearrange("p (k e) n -> p e k n", e=2)
            cm, i64 = cst("cmask"), cst("i64")
            for c in range(NC_):
                dve.wait_ge(c_tr, c + 1)
                if c == 0:
                    dve.memset(SV[0:CH, :, :], 0.0)
                for b in range(2):
                    src = bank(2 + b)[0:CH, :].rearrange("p (h n) -> p h n", h=8)
                    dve.tensor_copy(SV[CH:P, 8 * b:8 * b + 8, :], src)
                    dve.tensor_copy(UV[CH:P, 8 * b:8 * b + 8, :], src)
                dve.wait_ge(c_ps, 2 * c + 1)
                for e in range(2):
                    for b in range(2):
                        src = bank(4 + 2 * e + b).rearrange("p (k n) -> p k n", k=4)
                        dve.tensor_tensor(QS4[CH:P, e, 4 * b:4 * b + 4, :], src[CH:P], bc(cm[CH:P], CH, 4, P), ALU.mult)
                        ins = dve.tensor_tensor(MB4[0:CH, e, 4 * b:4 * b + 4, :], src[0:CH], bc(cm[0:CH], CH, 4, P),
                                                ALU.mult)
                link(ins)
                for e in range(2):
                    hp = HD * e
                    dve.tensor_tensor(Bf[2][hp:hp + HD], MB4[0:CH, e, :, 0:CH], bc(cst("omask")[0:CH], CH, 8, CH),
                                      ALU.mult)
                    ins = dve.tensor_tensor(Bf[0][hp:hp + HD], MB4[0:CH, e, :, 0:CH],
                                            bc(cst("dmask")[0:CH], CH, 8, CH), ALU.mult)
                link(ins)
                dve.tensor_tensor(Bf[3], Bf[0], bc(i64, P, 8, CH), ALU.add)
                dve.wait_ge(c_ps, 2 * c + 2)
                dve.tensor_tensor(Bf[1], bank(0).rearrange("p (k n) -> p k n", k=8), bc(cst("dtmask"), P, 8, CH),
                                  ALU.mult).then_inc(c_dve, 1)
                for n, step in enumerate(INVERSE):
                    dve.wait_ge(i_ps, NSTEP * c + n + 1)
                    done = EVA[NSTEP] * c + EVA[n]
                    for _, _, at, evs in step:
                        for engine, to in evs:
                            src = bank(at).rearrange("p (k n) -> p k n", k=8)
                            if engine == "act":
                                copied, done = Bf[to], done + 1
                            elif engine == "dve+":
                                dve.wait_ge(i_act, done)
                                dve.tensor_tensor(Bf[to], copied, bc(i64, P, 8, CH), ALU.add).then_inc(i_dve, 1)
                            elif (n, to) in PLUS_ID:
                                dve.tensor_tensor(Bf[to], src, bc(i64, P, 8, CH), ALU.add).then_inc(i_dve, 1)
                            else:
                                dve.tensor_copy(Bf[to], src).then_inc(i_dve, 1)
                dve.wait_ge(v_ps, c + 1)
                for e in range(2):
                    ins = dve.tensor_copy(UV4[0:CH, e, :, :], bank(4 + e)[0:CH, :].rearrange("p (k n) -> p k n", k=8))
                ins.then_inc(uv_ev, 1)
                if c == NC_ - 1:
                    break
                dve.wait_ge(n_ps, c + 1)
                for b in range(2):
                    src = bank(2 + b)[0:CH, :].rearrange("p (h n) -> p h n", h=8)
                    ins = dve.tensor_tensor(SV[0:CH, 8 * b:8 * b + 8, :], src, SV[0:CH, 8 * b:8 * b + 8, :], ALU.add)
                link(ins)
                dve.tensor_tensor(SV[0:CH], SV[0:CH],
                                  wendh[0:CH, :, c:c + 1].to_broadcast([CH, NH, CH]), ALU.mult).then_inc(st_ev, 1)

            def gn_finish(i):
                dve.wait_ge(gn_var, i + 1)
                v = sc[:, 2 + i % 2, :]
                link(dve.tensor_scalar(v, bank(4 + i % 2)[:, 0:T], 1.0 / HD, GN_EPS, ALU.mult, ALU.add))
                dve.reciprocal(v, v).then_inc(gn_rc, 1)
                dve.wait_ge(gn_rt, i + 1)
                y = yv[:, i, :, :]
                cut = lambda s: s.rearrange("p (n t) -> p n t", n=NC_)
                link(dve.scalar_tensor_tensor(out=y, in0=y, scalar=prm("lnw", i), in1=cut(sc[:, 4 + i % 2, :]),
                                              op0=ALU.mult, op1=ALU.mult))
                link(dve.scalar_tensor_tensor(out=y, in0=y, scalar=prm("lnb", i), in1=cut(bonT[:, i, :]),
                                              op0=ALU.add, op1=ALU.add))
                dve.tensor_tensor(cut(mixT[:, WT + i, :]), y, cut(gT[:, i, :]), ALU.mult).then_inc(gn_out, 1)

            dve.wait_ge(y_ev, NC_)
            for i in range(WT):
                dve.wait_ge(gn_mu, i + 1)
                mu = bank(i % 2)[:, 0:T].rearrange("p (n t) -> p n t", n=NC_)
                dve.scalar_tensor_tensor(out=yv[:, i, :, :], in0=mu, scalar=-1.0 / HD, in1=yv[:, i, :, :],
                                         op0=ALU.mult, op1=ALU.add).then_inc(gn_in, 1)
                if i:
                    gn_finish(i - 1)
            gn_finish(WT - 1)

            for c in range(DT):
                dve.wait_ge(w_used, BASE["out"] + c + 1)
                dve.tensor_tensor(xT[:, c, :], xT[:, c, :], bank(c % 2)[:, 0:T], ALU.add).then_inc(res_ready, 1)
            scale(1, "n2", uT)
            with dve.Fori(0, FT // 2) as i:
                for j in range(2):
                    dve.wait_ge(w_used, i * RING + (BASE["gu"] + 2 * j + 2))
                    dve.wait_ge(gs_ready, i * 2 + (j + 1))
                    dve.tensor_tensor(GT[:, bass.ds(i * 2 + j, 1), :], ps[:, 2 * j + 1:2 * j + 2, 0:T],
                                      GS[:, j:j + 1, :], ALU.mult).then_inc(gu_ev, 1)
            with dve.Fori(0, DT // 2) as i:
                for j in range(2):
                    dve.wait_ge(w_used, i * 8 + (BASE["down"] + 4 * j + 4))
                    dve.tensor_tensor(xT[:, bass.ds(i * 2 + j, 1), :], xT[:, bass.ds(i * 2 + j, 1), :],
                                      ps[:, j:j + 1, 0:T], ALU.add).then_inc(res_ready, 1)
            scale(2, "fg", xT)
            scale(3, "n1b", uT)
            C1 = 6.28125
            C2 = round((2 * math.pi - C1) * 2 ** 21) / 2 ** 21
            C3 = 2 * math.pi - C1 - C2
            MAGIC = 1.5 * 2 ** 23
            r0, r1 = ropt[:, 0, :], ropt[:, 1, :]
            dve.wait_ge(s_pos, 16)
            link(dve.tensor_copy(posf, r0.bitcast(I32)))
            link(dve.tensor_scalar(posf, posf, cst("invf"), None, ALU.mult))
            link(dve.tensor_scalar(r0, posf, 1 / (2 * math.pi), MAGIC, ALU.mult, ALU.add))
            link(dve.tensor_scalar(r0, r0, MAGIC, None, ALU.subtract))
            for part in (C1, C2, C3):
                link(dve.scalar_tensor_tensor(out=posf, in0=r0, scalar=-part, in1=posf, op0=ALU.mult, op1=ALU.add))
            link(dve.tensor_scalar(r1, posf, 3.1415925, -3.1415925, ALU.min, ALU.max))
            link(dve.tensor_scalar(r0, r1, -1.0, None, ALU.mult))
            link(dve.tensor_tensor(r0, r0, r1, ALU.max))
            dve.tensor_scalar(posf, r0, -1.0, math.pi / 2, ALU.mult, ALU.add).then_inc(sin_in, 1)
            link(dve.memset(HP[:, :, 0:PAD], 0.0))
            par_col = lambda at: par[:, bass.ds(at, 1)]
            one = lambda t, i, j: t[:, bass.ds(i * 2 + j, 1), :]
            with dve.Fori(0, WT // 2) as i:
                for j in range(2):
                    dve.wait_ge(sg_ready, i * 2 + (j + 1))
                    dve.scalar_tensor_tensor(out=HP[:, bass.ds(i * 2 + j, 1), PAD:PAD + T], in0=ps[:, 2 * j:2 * j + 1, 0:T],
                                             scalar=par_col(i * RING + (PAR["bin2"][0] + 2 * j)), in1=sg[:, j:j + 1, :],
                                             op0=ALU.add, op1=ALU.mult).then_inc(cv_ev, 1)
                dve.wait_ge(cv_ev, i * 2 + 2)
                for k in range(CONV_K):
                    for j in range(2):
                        w = par_col(i * (2 * CONV_K) + (PAR["cw"][0] + j * CONV_K + k))
                        src = HP[:, bass.ds(i * 2 + j, 1), k:k + T]
                        if k == 0:
                            dve.tensor_scalar(one(mix2, i, j), src, w, par_col(i * 2 + (PAR["cb"][0] + j)), ALU.mult,
                                              ALU.add).then_inc(tap, 1)
                        else:
                            dve.wait_ge(tap, i * (2 * CONV_K) + (2 * k + j - 1))
                            dve.scalar_tensor_tensor(out=one(mix2, i, j), in0=src, scalar=w, in1=one(mix2, i, j),
                                                     op0=ALU.mult, op1=ALU.add).then_inc(tap, 1)
            dve.wait_ge(sin_out, 1)

            def rotate(n):
                dve.wait_ge(q_rot, n + 1)
                a, b = qsc[:, 2, :], qsc[:, 3, :]
                dve.tensor_tensor(a, qnm[:, n % 2, :], cosT, ALU.mult)
                link(dve.tensor_tensor(b, bank(5)[:, 0:T], sinT, ALU.mult))
                dve.tensor_tensor(QR[:, n, :] if n < 8 else KR, a, b, ALU.add).then_inc(q_done, 1)
                dve.wait_ge(q_done, n + 1)

            for n in range(10):
                if n < 9:
                    dve.wait_ge(q_ss, n + 1)
                    if n:
                        dve.wait_ge(q_rt, n)
                    link(dve.tensor_scalar(qsc[:, 0, :], bank(4)[:, 0:T], 1.0 / HD, RMS_EPS, ALU.mult, ALU.add))
                    dve.reciprocal(qsc[:, 0, :], qsc[:, 0, :]).then_inc(q_rc, 1)
                    dve.wait_ge(q_rt, n + 1)
                    dve.scalar_tensor_tensor(out=qnm[:, n % 2, :], in0=qraw[:, n % 2, :],
                                             scalar=prm("qg" if n < 8 else "kg"), in1=qsc[:, 1, :],
                                             op0=ALU.mult, op1=ALU.mult).then_inc(q_nm, 1)
                if n:
                    rotate(n - 1)
            dve.wait_ge(ln_ps, 1)
            link(dve.tensor_scalar(nrm, bank(6)[:, 0:T], 1.0 / W, None, ALU.mult))
            dve.tensor_tensor(mix2[:, 0:WT, :], mix2[:, 0:WT, :], bc(nrm, P, WT, T), ALU.subtract).then_inc(ln_mid, 1)
            dve.wait_ge(ln_ps, 2)
            link(dve.tensor_scalar(nrm, bank(7)[:, 0:T], 1.0 / W, RMS_EPS, ALU.mult, ALU.add))
            dve.reciprocal(nrm, nrm).then_inc(ln_rc, 1)
            dve.wait_ge(ln_rt, 1)
            dve.tensor_tensor(mix2[:, 0:WT, :], mix2[:, 0:WT, :], bc(rstd, P, WT, T), ALU.mult).then_inc(ln_mul, 1)
            dve.wait_ge(s_sink, 16)

            def divide2(h):
                dve.wait_ge(ex2_ready, h + 1)
                s4 = small[:, 16 * (h % 2):16 * (h % 2) + 16]
                link(dve.tensor_tensor(s4[:, 4:6], s4[:, 4:6], s4[:, 8:10], ALU.add))
                link(dve.reciprocal(s4[:, 6:8], s4[:, 4:6]))
                dve.tensor_scalar(LG2[:, h % 2, 0:256], LG2[:, h % 2, 0:256], s4[:, 6:7], None, ALU.mult)
                dve.tensor_scalar(LG2[:, h % 2, 256:384], LG2[:, h % 2, 256:384], s4[:, 7:8], None, ALU.mult)\
                    .then_inc(pn2_ready, 1)

            for h in range(NH + 1):
                if h < NH:
                    dve.wait_ge(sc2_ps, h + 1)
                    if h >= 2:
                        dve.wait_ge(tp2_ps, h - 1)
                    dve.scalar_tensor_tensor(out=LG2[:, h % 2, :], in0=bank(2)[:, 0:384], scalar=HD ** -0.5,
                                             in1=cst("swa"), op0=ALU.mult, op1=ALU.add).then_inc(lg2_used, 1)
                    dve.wait_ge(lg2_used, h + 1)
                    s4 = small[:, 16 * (h % 2):16 * (h % 2) + 16]
                    dve.tensor_reduce(s4[:, 0:1], LG2[:, h % 2, 0:256], AX, ALU.max)
                    link(dve.tensor_reduce(s4[:, 1:2], LG2[:, h % 2, 256:384], AX, ALU.max))
                    dve.tensor_scalar(s4[:, 2:4], s4[:, 0:2], sinkr[:, h:h + 1], -1.0, ALU.max, ALU.mult)\
                        .then_inc(lg2_ready, 1)
                if h:
                    divide2(h - 1)
            for c in range(DT):
                dve.wait_ge(w_used, BASE["out2"] + c + 1)
                dve.tensor_tensor(xT[:, c, :], xT[:, c, :], bank(c % 2)[:, 0:T], ALU.add).then_inc(res_ready, 1)
            scale(4, "n2b", uT)

            def top16(values, best, index, work):
                link(dve.max(best[:, 0:8], values))
                dve.max_index(index[:, 0:8], best[:, 0:8], values)
                link(dve.match_replace(work, best[:, 0:8], values, -3.0e38))
                link(dve.max(best[:, 8:16], work))
                link(dve.max_index(index[:, 8:16], best[:, 8:16], work))

            it16 = cst("iota")[:, 0:TOPK]
            for t in range(2):
                dve.wait_ge(sub_ev, 8)
                for n in range(2 * PH):
                    top16(SUB[:, t, n, :], top[:, t, n, :], topi[:, t, n, :].bitcast(U32), wk[:, n % 2, 0:NK])
                link(dve.tensor_copy(topif[:, t, :, :], topi[:, t, :, :].bitcast(U32)))
                for h in range(PH):
                    c = cand[:, h % 2, :]
                    link(dve.tensor_tensor(c.rearrange("p (a b) -> p a b", a=TOPK),
                                           top[:, t, 2 * h, :].unsqueeze(2).to_broadcast([P, TOPK, TOPK]),
                                           top[:, t, 2 * h + 1, :].unsqueeze(1).to_broadcast([P, TOPK, TOPK]), ALU.add))
                    top16(c, val[:, t, h, :], vali[:, t, 0, h, :].bitcast(U32), wk[:, h % 2, :])
                v0, v1 = vali[:, t, 0, :, :].bitcast(U32), vali[:, t, 1, :, :].bitcast(U32)
                link(dve.tensor_scalar(v1, v0, 15, None, ALU.bitwise_and))
                link(dve.tensor_scalar(v0, v0, 4, None, ALU.logical_shift_right))
                link(dve.tensor_copy(valf[:, t, :, :, :], vali[:, t, :, :, :].bitcast(U32)))
                for h in range(PH):
                    for n in range(2):
                        p1 = pick[:, n, :, :]
                        link(dve.tensor_tensor(p1, valf[:, t, n, h, :].unsqueeze(2).to_broadcast([P, TOPK, TOPK]),
                                               it16.unsqueeze(1).to_broadcast([P, TOPK, TOPK]), ALU.is_equal))
                        link(dve.tensor_tensor(p1, p1, topif[:, t, 2 * h + n, :].unsqueeze(1)
                                               .to_broadcast([P, TOPK, TOPK]), ALU.mult))
                        link(dve.tensor_reduce(exs[:, t, n, h * TOPK:(h + 1) * TOPK], p1, AX, ALU.add))
                link(dve.tensor_copy(vsum[:, t, 0:PH].unsqueeze(2), val[:, t, :, 0:1]))
                dve.tensor_tensor(val[:, t, :, :], val[:, t, :, :],
                                  vsum[:, t, 0:PH].unsqueeze(2).to_broadcast([P, PH, TOPK]), ALU.subtract)\
                    .then_inc(soft_in, 1)
            for t in range(2):
                dve.wait_ge(soft_ex, t + 1)
                link(dve.tensor_reduce(vsum[:, t, 0:PH], val[:, t, :, :], AX, ALU.add))
                link(dve.reciprocal(vsum[:, t, PH:2 * PH], vsum[:, t, 0:PH]))
                dve.tensor_tensor(exs[:, t, 2, :].rearrange("p (h k) -> p h k", h=PH), val[:, t, :, :],
                                  vsum[:, t, PH:2 * PH].unsqueeze(2).to_broadcast([P, PH, TOPK]), ALU.mult)\
                    .then_inc(route_ready, 1)
            dve.wait_ge(et_ps, 1)
            for t in range(2):
                ins = dve.tensor_copy(eT[:, :, t * P:(t + 1) * P],
                                      bank(4 + t)[:, 0:3 * P].rearrange("p (n k) -> p n k", n=3))
            ins.then_inc(et_ev, 1)
            dve.wait_ge(et_ev, 1)

            def one_hots(i, b, first):
                if not first:
                    dve.wait_ge(g_ps, i * 2 + (b - 1))
                for t in range(4):
                    tok = lambda n: eT[:, n, bass.ds(i * 8 + (4 * b + t), 1)]
                    dve.tensor_scalar(OH[:, b, 0, t, :], cst("iota"), tok(0), tok(2), ALU.is_equal, ALU.mult)
                    ins = dve.tensor_scalar(OH[:, b, 1, t, :], cst("iota"), tok(1), None, ALU.is_equal)
                ins.then_inc(oh_ready, 1)

            def apply(i, b):
                dve.wait_ge(g_ps, i * 2 + (b + 1))
                h4 = HB[:, :, bass.ds(i * 8 + 4 * b, 4)].rearrange("p j t -> p t j")
                dve.tensor_tensor(h4, h4, bank(4 + b).rearrange("p (t j) -> p t j", t=4), ALU.mult)\
                    .then_inc(g_used, 1)

            one_hots(0, 0, True)
            one_hots(0, 1, True)
            dve.wait_ge(u_ev, NK)
            with dve.Fori(0, 31) as i:
                for b in range(2):
                    apply(i, b)
                    one_hots(i + 1, b, False)
            for b in range(2):
                apply(31, b)
            dve.wait_ge(w_used, BASE["v"] + NK)
            for b in range(8):
                ins = dve.tensor_copy(xT[:, 2 * b:2 * b + 2, :], bank(b).rearrange("p (c t) -> p c t", c=2))
                if b % 2:
                    ins.then_inc(y_ready, 1)


def chunks(w, kt=DT):
    k, n = w.shape
    q = k // (kt * P)
    return np.ascontiguousarray(w.reshape(q, kt, P, n // P, P).transpose(3, 0, 2, 1, 4).reshape(-1, P, kt * P))


def columns(v, tiles):
    v = np.asarray(v).reshape(-1)
    return v.reshape(tiles, P).T


def lay_out(x):
    f = lambda n: np.asarray(x[n])
    out = {"x": f("x")[0].T, "con": constants(), "dist": distance_constants(), "table": f("rel_bias_table"),
           "w_up": f("rwkv_w_up")[0], "a_up": f("rwkv_a_up")[0], "g_up": f("rwkv_g_up")[0]}
    w_in = f("w_in")[0]
    out["w_qkv"] = chunks(w_in[:, :3 * W])
    order = np.concatenate([np.arange(3 * W, 3 * W + 128)] +
                           [g * W + np.arange(i * P, (i + 1) * P) for i in range(WT) for g in range(3)])
    gate = 3 * W + 128 + np.arange(160)

    def z_columns(m):
        pad = np.zeros((m.shape[0], 96), np.float32)
        return np.concatenate([m[:, order[:128]], m[:, gate], pad, m[:, order[128:]]], 1)

    out["w_z"] = chunks(z_columns(w_in[:, 3 * W:]))
    mix = z_columns(f("rwkv_shift_mix"))[0]
    out["w_out"] = chunks(f("w_out")[0])
    gu = f("w_gate_up")[0].reshape(D, 2, FT, P).transpose(0, 2, 1, 3).reshape(D, 2 * FFN)
    out["w_gu"] = chunks(gu)
    out["w_down"] = chunks(f("w_down")[0], DOWN_KT)
    heads = np.array([h for i in range(8) for h in (i, i + 8)])
    q_cols = (heads[:, None] * HD + np.arange(HD)).reshape(-1)
    conv = np.arange(2 * W).reshape(2, WT, P).transpose(1, 0, 2).reshape(-1)
    cols = np.concatenate([conv, 2 * W + q_cols, np.arange(3 * W, 3 * W + 256)])
    out["w_in2"] = chunks(f("w_in_2")[:, cols])
    b_in = f("b_in_2")[cols]
    w_out2 = f("w_out_2")
    out["w_out2"] = chunks(np.concatenate([w_out2[:W], w_out2[W:][q_cols]], 0))
    out["b_v"] = b_in[-P:][None, :]
    out["sinks"] = f("attn_sinks_2")[heads][None, :]
    out["pos"] = f("positions_2")
    out["w_wq"] = chunks(f("peer_w_q_2"))
    out["keys"] = f("peer_sub_keys_2").transpose(3, 0, 1, 2).reshape(P, 2 * PH * NK)
    out["w_u"] = np.ascontiguousarray(f("peer_u_2").reshape(NK, NK, DT, P).transpose(1, 3, 2, 0)).reshape(NK, P, SLOT)
    out["w_v"] = f("peer_v_2").reshape(NK, NK, D)
    vec = {"n1": f("norm1_g"), "n2": f("norm2_g"), "fg": f("final_g"), "n1b": f("norm1_g_2"), "n2b": f("norm2_g_2"),
           "mix": mix, "w0": f("rwkv_w0"), "a0": f("rwkv_a0"), "kk": f("rwkv_k_k"), "ka": f("rwkv_k_a"),
           "rk": f("rwkv_r_k"), "lnw": f("rwkv_ln_w"), "lnb": f("rwkv_ln_b"), "bin2": b_in,
           "cb": f("conv_dw_b_2"), "clg": f("conv_ln_g_2"), "clb": f("conv_ln_b_2")}
    parts = []
    for name, n in PARAMS:
        if name == "cw":
            parts.append(f("conv_dw_w_2").reshape(CONV_K, WT, P).transpose(2, 1, 0).reshape(P, WT * CONV_K))
        elif name in ("qg", "kg"):
            g = f("q_norm_g_2" if name == "qg" else "k_norm_g_2")
            parts.append(np.concatenate([g, g])[:, None])
        else:
            parts.append(columns(vec[name], n))
    out["par"] = np.concatenate(parts, 1)
    return {k: np.ascontiguousarray(v) for k, v in out.items()}


def kernel(**inputs):
    import concourse.bacc as bacc
    from concourse.bass_utils import run_bass_kernel_spmd

    arrays = lay_out(inputs)
    nc = bacc.Bacc("TRN2", target_bir_lowering=False, num_devices=1)
    A = {k: nc.dram_tensor(k, a.shape, mybir.dt.from_np(a.dtype), kind="ExternalInput").ap()
         for k, a in arrays.items()}
    A["y"] = nc.dram_tensor("y", (D, T), F32, kind="ExternalOutput").ap()
    build(nc, A)
    r = run_bass_kernel_spmd(nc, [arrays], core_ids=[0])
    return np.ascontiguousarray(r.results[0]["y"].T).reshape(1, T, D)
```

```python
import math
from contextlib import ExitStack

import numpy as np

import concourse.bass as bass
from concourse import mybir

F32 = mybir.dt.float32
F32R = mybir.dt.float32r
BF16 = mybir.dt.bfloat16
I32 = mybir.dt.int32
U32 = mybir.dt.uint32
ALU = mybir.AluOpType
ACT = mybir.ActivationFunctionType
AX = mybir.AxisListType.X

P = 128
T = 256
D = 2048
DT = D // P
HD = 64
NH = 16
W = 1024
WT = W // P
FFN = 5632
FT = FFN // P
RING = 4
UKT = 8
SLOT = UKT * P
CH = 64
NC_ = T // CH
CONV_K = 31
NK = 128
PH = 8
TOPK = 16
RMS_EPS = 1e-6
GN_EPS = 64e-5
DECAY = math.exp(-0.5)
NEG = -1e30

QJ = 32
NQ = NK // QJ
DOWN_U = 6
V_U = QJ // UKT
EXPERT_U = 2 * QJ
assert EXPERT_U == DT * V_U == T // 4

STAGES = [("qkv", 48), ("z", 54), ("out", 32), ("gu", 176), ("down", 96), ("in2", 52), ("out2", 32), ("wq", 32)]
for _name in ("u0", "u1", "v0", "u2", "v1", "u3", "v2", "v3"):
    STAGES.append((_name, EXPERT_U))
BASE = {}
_at = 0
for _name, _n in STAGES:
    BASE[_name] = _at
    _at += _n
UNITS = _at

PARAMS = [("n1", 16), ("n2", 16), ("fg", 16), ("n1b", 16), ("n2b", 16), ("mix", 27), ("w0", 8), ("a0", 8),
          ("kk", 8), ("ka", 8), ("rk", 8), ("lnw", 8), ("lnb", 8), ("bin2", 26), ("cw", 8 * CONV_K), ("cb", 8),
          ("clg", 8), ("clb", 8), ("qg", 1), ("kg", 1)]
PAR = {}
_at = 0
for _name, _n in PARAMS:
    PAR[_name] = (_at, _n)
    _at += _n
NPAR = _at

CONSTS = [("ident", P), ("ones", P), ("blk", P), ("iota", P), ("cmask", P), ("reset", T),
          ("dmask", CH), ("omask", CH), ("dtmask", CH), ("i64", CH), ("swa", 384), ("perm", P), ("invf", 1)]
CON = {}
_at = 0
for _name, _n in CONSTS:
    CON[_name] = (_at, _n)
    _at += _n
NCON = _at
KEEP = 4 * P


def constants():
    p = np.arange(P)[:, None]
    f = np.arange(P)[None, :]
    c = {}
    c["ident"] = p == f
    c["ones"] = np.ones((P, P))
    c["blk"] = (p // HD) == (f // HD)
    c["iota"] = np.broadcast_to(f, (P, P))
    s, t = p % CH, f % CH
    c["cmask"] = np.where(f < CH, s < t, s <= t)
    c["reset"] = np.broadcast_to(np.arange(T)[None, :] % CH != 0, (P, T))
    pp, ff = p, np.arange(CH)[None, :]
    same = (pp % CH) // 16 == ff // 16
    c["dmask"] = (pp % CH < ff) & same
    c["omask"] = (pp % CH < ff) & ~same
    c["dtmask"] = (pp % CH > ff) & same
    c["i64"] = pp % CH == ff
    prev = np.where(f > p, 0.0, NEG)
    diag = np.where(f <= p, 0.0, NEG)
    c["swa"] = np.concatenate([prev, diag, diag], 1)
    perm = np.zeros((P, P))
    for h in (0, HD):
        for i in range(8):
            perm[h + 8 + i, h + i] = -1.0
            perm[h + i, h + 8 + i] = 1.0
    c["perm"] = perm
    inv = np.float32(500000.0) ** (-np.arange(0, 16, 2, dtype=np.float32) / np.float32(16))
    invf = np.zeros((P, 1))
    for h in (0, HD):
        invf[h:h + 8, 0] = inv
        invf[h + 8:h + 16, 0] = inv
    c["invf"] = invf
    return np.concatenate([np.broadcast_to(c[n], (P, k)).astype(np.float32) for n, k in CONSTS], 1)


def distance_constants():
    y = np.arange(384)
    d = 255 - y
    df = np.maximum(d, 1).astype(np.float32)
    large = 16 + (np.log(df / np.float32(16)) / np.float32(math.log(2048 / 16)) * np.float32(16)).astype(np.int32)
    bucket = np.where(d < 16, d, np.minimum(large, 31))
    hot = (np.arange(32)[:, None] == bucket[None, :]) & (d >= 0)[None, :]
    n = (d <= 128).astype(int) + (d % 4 == 0) + (d % 16 == 0)
    n = np.where(d >= 0, n, 0)
    ln = np.where(n > 0, np.log(np.maximum(n, 1)), NEG)
    return np.concatenate([hot.astype(np.float32), np.broadcast_to(ln, (16, 384)).astype(np.float32)], 0)


INVERSE = [
    [(1, 0, 0, [("act", 4)]),
     (0, 1, 1, [("act", 5), ("dve+", 6)])],
    [(5, 4, 2, [("act", 0)]),
     (4, 5, 3, [("act", 1), ("dve+", 3)]),
     (6, 3, 0, [("dve", 7)])],
    [(0, 1, 1, [("dve", 4)]),
     (3, 7, 2, [("act", 5)])],
    [(4, 5, 3, [("act", 0)])],
    [(0, "i", 0, [("dve", 1)])],
    [(1, 2, 1, [("act", 3)]),
     (2, 1, 2, [("act", 4), ("dve+", 6)])],
    [(3, 4, 3, [("dve", 5)])],
    [(5, 0, 0, [("act", 7)])],
    [(6, 7, 1, [("dve", 8)])],
]
PLUS_ID = {(2, 4), (6, 5)}
NSTEP = len(INVERSE)


def evacuations(engine):
    counts = [0]
    for step in INVERSE:
        counts.append(counts[-1] + sum(e.startswith(engine) for _, _, _, ev in step for e, _ in ev))
    return counts


EVA, EVD = evacuations("act"), evacuations("dve")
GROUPS = 2


def evacuated(counts, chunk, step, group=GROUPS - 1):
    before = counts[max(step - 1, 0)]
    return GROUPS * (counts[NSTEP] * chunk + before) + (group + 1) * (counts[step] - before)


def build(nc, A):
    ctx = ExitStack()
    with ctx:
        def sem(name):
            return ctx.enter_context(nc.semaphore(name))

        def sb(name, width, dt=F32):
            return nc.sbuf_tensor(name, [P, width], dt)

        xT_ = ctx.enter_context(sb("xT", DT * T))
        with sb("under_uh", DT * T) as ua_, sb("under_ul", DT * T) as ub_:
            pass
        uh_ = ctx.enter_context(sb("uh", DT * T, F32R))
        ul_ = ctx.enter_context(sb("ul", DT * T, F32R))
        raw_ = ctx.enter_context(sb("raw", RING * SLOT))
        wh_ = ctx.enter_context(sb("wh", RING * SLOT, F32R))
        wl_ = ctx.enter_context(sb("wl", RING * SLOT, F32R))
        par = ctx.enter_context(sb("params", NPAR))
        con = ctx.enter_context(sb("consts", KEEP))
        misc = ctx.enter_context(sb("misc", 2560))
        with sb("gh", FT * T, F32R) as gh_, sb("gl", FT * T, F32R) as gl_:
            pass
        with sb("eh", QJ * T, F32R) as eh_, sb("el1", QJ * T, F32R) as el1_, sb("el0", QJ * T, F32R) as el0_:
            pass
        ARENA = 25088
        arena = ctx.enter_context(sb("arena", ARENA))
        ps = ctx.enter_context(nc.psum_tensor("ps", [P, 8, 512], F32))
        dist_dram = nc.dram_tensor("dist_dram", [NH, P, 384], F32).ap()

        def view(tensor, at, *shape):
            n = int(np.prod(shape))
            v = tensor[:, at:at + n]
            if len(shape) == 2:
                return v.rearrange("p (a b) -> p a b", a=shape[0])
            if len(shape) == 3:
                return v.rearrange("p (a b c) -> p a b c", a=shape[0], b=shape[1])
            if len(shape) == 4:
                return v.rearrange("p (a b c d) -> p a b c d", a=shape[0], b=shape[1], c=shape[2])
            return v

        def bank(b):
            return ps[:, b, :]

        def prm(name, i=0):
            return par[:, PAR[name][0] + i:PAR[name][0] + i + 1]

        def cst(name):
            at, n = CON[name]
            return con[:, at:at + n] if at < KEEP else arena[:, at - KEEP:at - KEEP + n]

        xT, ua, ub, uh, ul = (view(m, 0, DT, T) for m in (xT_, ua_, ub_, uh_, ul_))
        raw, wh, wl = (view(m, 0, RING, SLOT) for m in (raw_, wh_, wl_))
        gh, gl = (view(m, 0, FT, T) for m in (gh_, gl_))
        ident, ones, blk = cst("ident"), cst("ones"), cst("blk")
        TAIL = NCON - KEEP
        rstd = misc[:, 0:T]
        nrm = misc[:, T:2 * T]

        small = misc[:, 2432:2560]
        LR2 = misc[:, 1408:1408 + W]
        VN = view(xT_, 0, 2, W)
        LR = view(xT_, 2 * W, 2, W)
        o = TAIL
        QK = view(arena, o, 16, T); o += 16 * T
        vT, gT = QK[:, 0:WT, :], QK[:, WT:2 * WT, :]
        temps = o
        BC = view(arena, o, 2, 384); o += 768
        LG = view(arena, o, 2, 384); o += 768
        PT = view(arena, o, 2, 384); o += 768
        lo = view(arena, o, 3, T); o += 3 * T
        zraw = view(arena, o, 2, T + 1); o += 2 * (T + 1)
        zdif = view(arena, o, T); o += T
        sc = view(arena, o, 12, T); o += 12 * T
        temps_end = o
        wend = view(arena, o, WT, NC_); o += WT * NC_
        wendh = view(arena, o, NH, NC_); o += NH * NC_
        attnT = view(arena, o, WT, T); o += WT * T
        bonT = view(arena, o, WT, T); o += WT * T
        sq1 = view(arena, o - 2 * WT * T, DT, T)
        AR = view(arena, o, WT, NC_, P); o += WT * NC_ * P
        BK = view(arena, o, WT, NC_, P); o += WT * NC_ * P
        yv = BK[:, :, :, 0:CH]
        assert o <= ARENA, o
        o = temps
        QS = view(arena, o, NH, P); o += NH * P
        MB = view(arena, o, NH, P); o += NH * P
        assert o <= temps_end, (o, temps_end)
        SV = view(xT_, 0, NH, CH)
        UV = view(xT_, 1024, NH, CH)
        BKn = view(xT_, 2048, NH, CH)
        Bf = [view(ua_, 512 * i, 8, CH) for i in range(8)] + [view(xT_, 3072, 8, CH)]

        GS = view(misc, 1024, 2, T)

        o = TAIL
        mix2 = view(arena, o, DT, T); o += DT * T
        PAD = CONV_K - 1
        HP = view(arena, o, WT, T + PAD); o += WT * (T + PAD)
        HS = view(arena, o - WT * (T + PAD), WT, T)
        QR = view(arena, o, WT, T); o += WT * T
        KR = view(arena, o, T); o += T
        VB = view(arena, o, 2, P); o += 2 * P
        LG2 = view(arena, o, 2, 384); o += 768
        PT2 = view(arena, o, 2, 384); o += 768
        sg = view(arena, o, 2, T); o += 2 * T
        qraw = view(arena, o, 2, T); o += 2 * T
        qsq = view(arena, o, 2, T); o += 2 * T
        qnm = view(arena, o, 2, T); o += 2 * T
        qsc = view(arena, o, 4, T); o += 4 * T
        posf = view(arena, o, T); o += T
        cosT = view(arena, o, T); o += T
        sinT = view(arena, o, T); o += T
        ropt = view(arena, o, 2, T); o += 2 * T
        sinkr = view(arena, o, NH); o += NH
        vT2 = view(arena, o, T); o += T
        E1, E0 = QJ * T, 2 * QJ * T
        assert o <= E0, o
        KEYS = view(arena, E0, 2 * PH * NK)
        HQ = view(arena, 0, DT, T)
        SUB = view(arena, DT * T, 2, 2 * PH, NK)
        o = 0
        wk = view(arena, o, 2, T); o += 2 * T
        cand = view(arena, o, 2, T); o += 2 * T
        top = view(arena, o, 2, 2 * PH, TOPK); o += 2 * 2 * PH * TOPK
        topi = view(arena, o, 2, 2 * PH, TOPK); o += 2 * 2 * PH * TOPK
        topif = view(arena, o, 2, 2 * PH, TOPK); o += 2 * 2 * PH * TOPK
        val = view(arena, o, 2, PH, TOPK); o += 2 * PH * TOPK
        vali = view(arena, o, 2, 2, PH, TOPK); o += 4 * PH * TOPK
        valf = view(arena, o, 2, 2, PH, TOPK); o += 4 * PH * TOPK
        vsum = view(arena, o, 2, 2 * PH); o += 4 * PH
        assert o <= DT * T, o
        eT = view(misc, 2 * T, 3, T)
        exs = view(misc, 5 * T, 2, 3, P)
        pick = view(misc, 8 * T, 2, TOPK, TOPK)
        half = lambda at, *shape: view(misc[:, at:at + int(np.prod(shape)) // 2].bitcast(BF16), 0, *shape)
        ROWS = half(5 * T, 2, 4, P)
        COLS = half(7 * T, 2, 4, 3 * QJ)
        HITS = half(7 * T + 384, 2, 4, QJ)
        GP = half(0, T, 3)
        SUMS = view(misc, 9 * T, 2, 4, QJ)
        rest = view(misc, 9 * T - 64, T)
        HB = [view(arena, (E0, E1)[q % 2], QJ, T) for q in range(NQ)]
        EL = [view((el0_, el1_)[q % 2], 0, QJ, T) for q in range(NQ)]
        EH = view(eh_, 0, QJ, T)

        def e_hi(q, j, n=1):
            if q < NQ - 1:
                return EH[:, j:j + n, :]
            return uh[:, j:j + n, :] if j < DT else ul[:, j - DT:j - DT + n, :]

        Q0, C0 = BASE["in2"], BASE["in2"] + 20
        CONV_BANKS = (0, 1, 5, 6)
        odd_taps = qsc[:, 2, :]

        s_con3, s_keys, s_pos, s_sink, s_y, vt_ready, v_ps2 = (sem(n) for n in (
            "con3_in", "keys_in", "pos_in", "sinks_in", "y_out", "vt_ready", "v_turned_ps"))
        (sg_ready, cv_ev, tap, sin_in, sin_out, q_raw, q_ss, q_rc, q_rt, q_nm, q_rot, q_done,
         v_ev, sc2_ps, lg2_used, lg2_ready, ex2_ready, pn2_ready, tp2_ps, pt2_ready, o2_ps, o2_ev, ln_ps, ln_mid,
         ln_sq, ln_rc, ln_rt, ln_mul, ln_out, wq_ev, sub_ps, sub_ev, u_ev, soft_in, soft_ex, route_ready, et_ps,
         et_ev, hits_ready, sums_ready, oh_ready, g_ps, gated, eh_ready, el_ready) = (sem(n) for n in (
            "sg_ready", "conv_in_ready", "tap", "sin_in", "sin_out", "q_raw", "q_ss",
            "q_rc", "q_rt", "q_normed", "q_rot", "q_done", "v_ev", "scores2_ps", "logits2_out", "logits2_ready",
            "exp2_ready", "probs2_ready", "transposed2_ps", "pt2_ready", "o2_ps", "o2_ev", "ln_ps", "ln_mid", "ln_sq",
            "ln_rc", "ln_rt", "ln_mul", "ln_out", "wq_ev", "sub_ps", "sub_ev", "experts_in", "soft_in", "soft_ex",
            "route_ready", "et_ps", "et_ev", "hits_ready", "sums_ready", "onehot_ready", "gates_ps", "gated",
            "expert_hi", "expert_lo"))

        w_in = [sem(f"w_in{s}") for s in range(RING)]
        hi_ready, lo_ready = sem("w_hi"), sem("w_lo")
        w_used = sem("w_used")
        p_ready, uh_ready = sem("p_ready"), sem("uh_ready")
        gp_ready, gh_ready, s_x2 = sem("gp_ready"), sem("gh_ready"), sem("x2_in")
        mh_ready, ml_ready = sem("mixed_hi"), sem("mixed_lo")
        s_x = [sem(f"x_in{k}") for k in range(4)]
        z_pad = sem("z_pad")
        s_par, s_con, s_con2, s_tab, s_lr, s_dist = (sem(n) for n in (
            "par_in", "con_in", "con2_in", "tab_in", "lowrank_in", "dist_out"))
        sq_ready, ss_ready, rs_ready, rstd_ready, u_ready, res_ready = (sem(n) for n in (
            "sq_ready", "ss_ready", "rs_ready", "rstd_ready", "u_ready", "res_ready"))
        dve_own, act_own = sem("dve_own"), sem("act_own")
        qkv_ev, z_raw, z_ready, low_ready = sem("qkv_ev"), sem("z_raw"), sem("z_ready"), sem("low_ready")
        dist_ps, dist_sb = sem("dist_ps"), sem("dist_sb")
        bc_in, bc_used = [sem("bc_in0"), sem("bc_in1")], sem("bc_used")
        sc_ps, lg_ready, ex_ready, pn_ready, tp_ps, pt_ready, o_ps, o_ev = (sem(n) for n in (
            "scores_ps", "logits_ready", "exp_ready", "probs_ready", "transposed_ps", "pt_ready", "o_ps", "o_ev"))
        lr_ps, lr_act, g_ev, kk_sq, ss_kk, kk_rc, kk_rt, bo_in, bo_ps, bo_used, lc_ready, e_ready = (
            sem(n) for n in ("lowrank_ps", "lowrank_act", "g_ev", "kk_sq", "kk_ss", "kk_rc", "kk_rt", "bonus_in",
                             "bonus_ps", "bonus_used", "logdecay_ready", "exps_ready"))
        v_copied, c_ps, c_tr, c_dve, c_act, i_ps, i_act, i_dve, r_ps, r_ev, v_ps, y_ps, n_ps, uv_ev, st_ev, y_ev = (
            sem(n) for n in ("v_copied", "c_ps", "c_tr", "c_dve", "c_act", "inv_ps", "inv_act", "inv_dve", "rhs_ps",
                             "rhs_ev",
                             "u_ps", "y_ps", "state_ps", "u_ev", "state_ev", "y_ev"))
        gu_ev, gs_ready, gn_in, gn_mu, gn_sq, gn_var, gn_rc, gn_rt, gn_out = (sem(n) for n in (
            "gu_ev", "silu_ready", "gn_in", "gn_mu", "gn_sq", "gn_var", "gn_rc", "gn_rt", "gn_out"))

        block = ctx.enter_context(nc.Block())

        @block.sync
        def _(sp):
            def stream(name, dram, at=0):
                n, base = dict(STAGES)[name], BASE[name]
                period = 2 * DOWN_U if name == "down" else RING
                width = lambda j: SLOT // 2 if name == "down" and j % DOWN_U == DOWN_U - 1 else SLOT

                def one(g, j):
                    slot = (base + j) % RING
                    sp.dma_start(raw[:, slot, 0:width(j)],
                                 dram[bass.ds(g, 1), :, 0:width(j)].rearrange("a p n -> p (a n)"))\
                        .then_inc(w_in[slot], 16)

                head = RING if base == 0 else 0
                for j in range(head):
                    one(at + j, j)
                turns = n // period
                with sp.Fori(head // RING, turns) as i:
                    for j in range(period):
                        sp.wait_ge(lo_ready, i * period + (base + j - RING + 1))
                        one(i * period + (at + j), j)
                for j in range(turns * period, n):
                    sp.wait_ge(lo_ready, base + j - RING + 1)
                    one(at + j, j)

            for name, _ in STAGES:
                if name[:-1] in ("u", "v"):
                    stream(name, A["w_" + name[0]], int(name[1]) * EXPERT_U)
                else:
                    stream(name, A["w_" + name])
            for c in range(0, DT, 4):
                sp.wait_ge(res_ready, (3 + NQ - 1) * DT + c + 4)
                sp.dma_start(A["y"].rearrange("(c p) t -> p c t", p=P)[:, c:c + 4, :],
                             xT[:, c:c + 4, :]).then_inc(s_y, 16)
            sp.wait_ge(s_y, 64)


        @block.gpsimd
        def _(pool):
            def split(g, slot, width=SLOT):
                pool.wait_ge(hi_ready, g)
                pool.tensor_tensor(wl[:, slot, 0:width], raw[:, slot, 0:width],
                                   wh[:, slot, 0:width].bitcast(F32), ALU.subtract).then_inc(lo_ready, 1)

            def splits(base, n, period=RING, narrow=()):
                with pool.Fori(0, n // period) as i:
                    for j in range(period):
                        split(i * period + (base + j + 1), (base + j) % RING, SLOT // 2 if j in narrow else SLOT)

            splits(0, 24)
            pool.wait_ge(dist_sb, 1)
            pool.dma_start(dist_dram, misc[0:NH, 1024:1408].unsqueeze(1).to_broadcast([NH, P, 384]))\
                .then_inc(s_dist, 16)
            pool.wait_ge(u_ready, DT)
            pool.dma_start(LR[0:64, 0, :], A["w_up"]).then_inc(s_lr, 16)
            pool.dma_start(LR[64:128, 0, :], A["a_up"]).then_inc(s_lr, 16)
            pool.dma_start(LR[:, 1, :], A["g_up"][0:P, :]).then_inc(s_lr, 16)
            pool.dma_start(LR2[0:32, :], A["g_up"][P:P + 32, :]).then_inc(s_lr, 16)
            splits(24, 24)

            def bias(h):
                if h == 0:
                    pool.wait_ge(s_dist, 16)
                if h >= 2:
                    pool.wait_ge(bc_used, h - 1)
                row = dist_dram[h, 0:1, 127:128]
                two = bass.AP(tensor=row.tensor, offset=row.offset, ap=[[383, P], [1, 256]])
                one = bass.AP(tensor=row.tensor, offset=row.offset + 128, ap=[[383, P], [1, 128]])
                pool.dma_start(BC[:, h % 2, 0:256], two).then_inc(bc_in[h % 2], 16)
                pool.dma_start(BC[:, h % 2, 256:384], one).then_inc(bc_in[h % 2], 16)

            for c in range(27):
                if c < NH:
                    bias(c)
                for j in range(2):
                    g = BASE["z"] + 2 * c + j
                    split(g + 1, g % RING)
            splits(BASE["out"], 32 + 176)
            splits(BASE["down"], 96, 2 * DOWN_U, (DOWN_U - 1, 2 * DOWN_U - 1))
            splits(BASE["in2"], 4)
            pool.wait_ge(u_ready, 3 * DT)
            pool.dma_start(arena[:, 0:TAIL], A["con"][:, KEEP:NCON]).then_inc(s_con3, 16)
            pool.dma_start(ropt[:, 0, :].bitcast(I32), A["pos"].to_broadcast([P, T])).then_inc(s_pos, 16)
            pool.dma_start(sinkr, A["sinks"].to_broadcast([P, NH])).then_inc(s_sink, 16)
            pool.dma_start(KEYS, A["keys"]).then_inc(s_keys, 16)
            splits(BASE["in2"] + 4, UNITS - BASE["in2"] - 4)


        @block.tensor
        def _(pe):
            def unit(out, ready, slot, xh, xl, kt=UKT, first=True, last=True):
                pe.wait_ge(lo_ready, ready)
                for c in range(kt):
                    at = slice(c * P, (c + 1) * P)
                    for n, (w, x) in enumerate(((wh, xh), (wh, xl), (wl, xh))):
                        ins = pe.matmul(out, w[:, slot, at], x(c), start=first and c == n == 0,
                                        stop=last and c == kt - 1 and n == 2)
                return ins

            def tile(out, g, slot, xh, xl, second=None):
                for n in range(2):
                    if n and second:
                        pe.wait_ge(*second)
                    unit(out, g + (n + 1), (slot + n) % RING, lambda c: xh(UKT * n + c), lambda c: xl(UKT * n + c),
                         first=n == 0, last=n == 1).then_inc(w_used, 1)

            def norm_sum(m, sq):
                for c in range(DT):
                    pe.wait_ge(sq_ready, DT * m + c + 1)
                    ins = pe.matmul(bank(2)[:, 0:T], ones, sq[:, c, :], start=c == 0, stop=c == DT - 1)
                ins.then_inc(ss_ready, 1)
                pe.wait_ge(u_ready, DT * m + UKT)

            def loop(name, at, tiles, evac, before):
                g0 = BASE[name] + 2 * at
                with pe.Fori(0, tiles // 4) as i:
                    for j in range(4):
                        pe.wait_ge(evac, i * 4 + (before + at + j - 1))
                        tile(bank((at + j) % 2)[:, 0:T], i * 8 + (g0 + 2 * j), (g0 + 2 * j) % RING, uhc, ulc)

            uhc = lambda c: uh[:, c, :]
            ulc = lambda c: ul[:, c, :]
            pe.wait_ge(s_con, 16)
            pe.wait_ge(s_tab, 32)
            pe.matmul(bank(3)[0:NH, 0:384], misc[0:32, 512:528], misc[0:32, 640:1024], start=True, stop=True)\
                .then_inc(dist_ps, 1)
            norm_sum(0, ua)
            for j in range(4):
                if j >= 2:
                    pe.wait_ge(qkv_ev, j - 1)
                tile(bank(j % 2)[:, 0:T], 2 * j, 2 * j % RING, uhc, ulc, None if j else (u_ready, DT))
            loop("qkv", 4, 12, qkv_ev, 0)
            pe.wait_ge(qkv_ev, 16)
            with pe.Fori(0, 2) as i:
                for j in range(2):
                    pe.wait_ge(qkv_ev, i * 4 + (2 * j + 14))
                    for n in range(RING):
                        pe.wait_ge(lo_ready, i * 8 + (32 + 4 * j + n + 1))
                        for t in range(2):
                            for c in range(4):
                                at = slice(c * T, (c + 1) * T)
                                for m, (x, w) in enumerate(((uh, wh), (ul, wh), (uh, wl))):
                                    ins = pe.matmul(bank(2 * j + t)[:, 0:T], x[:, 4 * n + c, t * P:(t + 1) * P],
                                                    w[:, n, at], start=n == c == m == 0,
                                                    stop=n == c == 3 and m == 2)
                        ins.then_inc(w_used, 1)

            def scores(h, q, k, done):
                hp = HD * (h % 2)
                out = bank(2)
                pe.matmul(out[:, 0:256], q[hp:hp + HD, P:T], k[hp:hp + HD, :], start=True, stop=True)
                pe.matmul(out[:, 256:384], q[hp:hp + HD, 0:P], k[hp:hp + HD, 0:P], start=True, stop=True)\
                    .then_inc(done, 1)

            def turn_probs(h, probs, done):
                for b in range(3):
                    ins = pe.transpose(bank(3)[:, b * P:(b + 1) * P], probs[:, b * P:(b + 1) * P], ident)
                ins.then_inc(done, 1)

            def weigh_v(h, v, pt, done):
                hp = HD * (h % 2)
                out = bank(4)[hp:hp + HD, 0:T]
                pe.matmul(out[:, P:T], v(0), pt[:, 0:P], start=True, stop=False)
                pe.matmul(out[:, P:T], v(1), pt[:, P:2 * P], start=False, stop=True)
                pe.matmul(out[:, 0:P], v(0), pt[:, 2 * P:3 * P], start=True, stop=True).then_inc(done, 1)

            def lowrank(i):
                col = slice(i * P, (i + 1) * P)
                if i == 0:
                    pe.wait_ge(low_ready, 3)
                    pe.wait_ge(s_lr, 64)
                else:
                    pe.wait_ge(lr_act, 2 * i)
                    pe.wait_ge(g_ev, i)
                pe.matmul(bank(6)[:, 0:T], LR[0:64, 0, col], lo[0:64, 0, :], start=True, stop=True)
                pe.matmul(bank(7)[:, 0:T], LR[:, 1, col], lo[:, 1, :], start=True, stop=False)
                pe.matmul(bank(7)[:, 0:T], LR2[0:32, col], lo[0:32, 2, :], start=False, stop=True)
                pe.matmul(bank(7)[:, T:2 * T], LR[64:128, 0, col], lo[64:128, 0, :], start=True, stop=True)\
                    .then_inc(lr_ps, 1)

            def key_sums(i):
                pe.wait_ge(kk_sq, i + 1)
                if i:
                    pe.wait_ge(bo_used, i)
                pe.matmul(bank(5)[:, 0:T], blk, sc[:, 5, :], start=True, stop=True).then_inc(ss_kk, 1)

            def bonus_sums(i):
                pe.wait_ge(bo_in, i + 1)
                pe.wait_ge(kk_rc, i + 1)
                pe.matmul(bank(5)[:, 0:T], blk, sc[:, 6, :], start=True, stop=True).then_inc(bo_ps, 1)

            for c in range(28):
                if c < 27:
                    g = BASE["z"] + 2 * c
                    if c < 2:
                        pe.wait_ge(qkv_ev, 22)
                    else:
                        pe.wait_ge(z_raw, c - 1)
                    tile(bank(c % 2)[:, 0:T], g, g % RING, uhc, ulc)
                if c >= 6 and c % 3 == 0:
                    key_sums(c // 3 - 2)
                if c < NH:
                    if c == 0:
                        pe.wait_ge(qkv_ev, 24)
                    if c:
                        pe.wait_ge(bc_used, c)
                    scores(c, QK[:, c // 2, :], QK[:, 8 + c // 2, :], sc_ps)
                if 1 <= c <= NH:
                    pe.wait_ge(pn_ready, c)
                    if c >= 2:
                        pe.wait_ge(pt_ready, c - 1)
                    turn_probs(c - 1, LG[:, (c - 1) % 2, :], tp_ps)
                if 2 <= c <= NH + 1:
                    h = c - 2
                    pe.wait_ge(pt_ready, h + 1)
                    if h >= 2 and h % 2 == 0:
                        pe.wait_ge(o_ev, h // 2)
                    weigh_v(h, lambda s, h=h: VN[:, s, h * HD:(h + 1) * HD], PT[:, h % 2, :], o_ps)
                if c >= 6 and c % 3 == 0:
                    bonus_sums(c // 3 - 2)
                if 3 <= c < 27 and c % 3 == 0:
                    lowrank(c // 3 - 1)

            for c in range(NC_):
                if c == 0:
                    pe.wait_ge(bo_used, WT)
                if c:
                    pe.wait_ge(y_ev, c)
                    pe.wait_ge(st_ev, c)
                for i in range(WT):
                    pe.transpose(bank(i // 4)[:, (i % 4) * P:(i % 4 + 1) * P], BK[:, i, c, :], ident)
                for i in range(WT):
                    ins = pe.transpose(bank(2 + i // 4)[0:CH, (i % 4) * P:(i % 4 + 1) * P],
                                       vT[:, i, c * CH:(c + 1) * CH], ident)
                ins.then_inc(c_tr, 1)
                for e in range(2):
                    hp = HD * e
                    for k in range(8):
                        ins = pe.matmul(bank(4 + 2 * e + k // 4)[:, (k % 4) * P:(k % 4 + 1) * P],
                                        BK[hp:hp + HD, k, c, :], AR[hp:hp + HD, k, c, :], start=True, stop=True)
                    ins.then_inc(c_ps, 1)
                pe.wait_ge(c_act, 5 * c + 2)
                for h in range(NH):
                    hp = HD * (h % 2)
                    k = h // 2
                    ins = pe.matmul(bank(0)[hp:hp + HD, k * CH:(k + 1) * CH], AR[hp:hp + HD, k, c, 0:CH],
                                    BK[hp:hp + HD, k, c, 0:CH], start=True, stop=True)
                ins.then_inc(c_ps, 1)
                for n, step in enumerate(INVERSE):
                    if n == 0:
                        pe.wait_ge(c_dve, c + 1)
                        pe.wait_ge(c_act, 5 * c + 5)
                    for g in range(GROUPS):
                        if evacuated(EVA, c, n, g):
                            pe.wait_ge(i_act, evacuated(EVA, c, n, g))
                        if evacuated(EVD, c, n, g):
                            pe.wait_ge(i_dve, evacuated(EVD, c, n, g))
                        for a, b, at, _ in step:
                            for h in range(8 * g, 8 * g + 8):
                                hp, k = HD * (h % 2), h // 2
                                rhs = cst("i64")[hp:hp + HD, :] if b == "i" else Bf[b][hp:hp + HD, k, :]
                                ins = pe.matmul(bank(at + 4 * g)[hp:hp + HD, k * CH:(k + 1) * CH],
                                                Bf[a][hp:hp + HD, k, :], rhs, start=True, stop=True)
                        ins.then_inc(i_ps, 1)
                pe.wait_ge(i_dve, evacuated(EVD, c, NSTEP))
                pe.wait_ge(i_act, evacuated(EVA, c, NSTEP))
                for g in range(GROUPS):
                    for h in range(8 * g, 8 * g + 8):
                        hp, k = HD * (h % 2), h // 2
                        ins = pe.matmul(bank(g)[hp:hp + HD, k * CH:(k + 1) * CH], QS[:, h, 0:CH], SV[:, h, :],
                                        start=True, stop=True)
                    ins.then_inc(r_ps, 1)
                for g in range(GROUPS):
                    pe.wait_ge(r_ev, GROUPS * c + g + 1)
                    for h in range(8 * g, 8 * g + 8):
                        hp, k = HD * (h % 2), h // 2
                        ins = pe.matmul(bank(4 - 2 * g + h % 2)[0:CH, k * CH:(k + 1) * CH], Bf[8][hp:hp + HD, k, :],
                                        Bf[3][hp:hp + HD, k, :], start=True, stop=True)
                    ins.then_inc(v_ps, 1)
                for g in range(GROUPS):
                    pe.wait_ge(uv_ev, GROUPS * c + g + 1)
                    for h in range(8 * g, 8 * g + 8):
                        hp, k = HD * (h % 2), h // 2
                        out = bank(6)[hp:hp + HD, k * CH:(k + 1) * CH]
                        pe.matmul(out, SV[:, h, :], QS[:, h, CH:P], start=True, stop=False)
                        ins = pe.matmul(out, UV[0:CH, h, :], MB[0:CH, h, CH:P], start=False, stop=True)
                ins.then_inc(y_ps, 1)
                for h in range(NH) if c < NC_ - 1 else ():
                    ins = pe.matmul(bank(2 + h // 8)[0:CH, (h % 8) * CH:(h % 8 + 1) * CH], BKn[:, h, :],
                                    UV[:, h, :], start=True, stop=True)
                if c < NC_ - 1:
                    ins.then_inc(n_ps, 1)

            for i in range(WT):
                if i == 0:
                    pe.wait_ge(y_ev, NC_)
                if i >= 2:
                    pe.wait_ge(gn_in, i - 1)
                pe.matmul(bank(i % 2)[:, 0:T], blk, yv[:, i, :, :], start=True, stop=True).then_inc(gn_mu, 1)
                if i:
                    pe.wait_ge(gn_sq, i)
                    if i >= 3:
                        pe.wait_ge(gn_rc, i - 2)
                    pe.matmul(bank(4 + (i - 1) % 2)[:, 0:T], blk, sc[:, (i - 1) % 2, :], start=True, stop=True)\
                        .then_inc(gn_var, 1)
            pe.wait_ge(gn_sq, WT)
            pe.matmul(bank(5)[:, 0:T], blk, sc[:, 1, :], start=True, stop=True).then_inc(gn_var, 1)

            pe.wait_ge(ml_ready, 2)
            for c in range(DT):
                g = BASE["out"] + 2 * c
                if c >= 2:
                    pe.wait_ge(res_ready, c - 1)
                tile(bank(c % 2)[:, 0:T], g, g % RING, uhc, ulc, None if c else (ml_ready, 2 + WT))
            norm_sum(1, sq1)
            g0 = BASE["gu"]

            def gate_up(i, first):
                for j in range(4):
                    if not first:
                        pe.wait_ge(gp_ready, i * 2 + (j // 2 - 1))
                    tile(bank(j)[:, 0:T], i * 8 + (g0 + 2 * j), (g0 + 2 * j) % RING, uhc, ulc,
                         (u_ready, 2 * DT) if first and j == 0 else None)

            gate_up(0, True)
            with pe.Fori(1, FT // 2) as i:
                gate_up(i, False)
            g0d = BASE["down"]
            pe.wait_ge(gu_ev, FT)
            with pe.Fori(0, DT // 2) as i:
                for t in range(2):
                    pe.wait_ge(res_ready, i * 2 + (DT + t - 1))
                    for q in range(DOWN_U):
                        j = DOWN_U * t + q
                        unit(bank(t)[:, 0:T], i * 2 * DOWN_U + (g0d + j + 1), (g0d + j) % RING,
                             lambda c: gh[:, UKT * q + c, :], lambda c: gl[:, UKT * q + c, :],
                             min(UKT, FT - UKT * q), q == 0, q == DOWN_U - 1).then_inc(w_used, 1)
            norm_sum(2, ua)
            norm_sum(3, ua)
            pe.wait_ge(s_con3, 16)
            for n in range(12):
                g = Q0 + 2 * n
                if n < 10:
                    if n >= 2:
                        pe.wait_ge(q_raw, n - 1)
                    tile(bank(n % 2)[:, 0:T], g, g % RING, uhc, ulc, None if n else (u_ready, 4 * DT))
                if 1 <= n <= 9:
                    m = n - 1
                    pe.wait_ge(q_raw, m + 1)
                    if m:
                        pe.wait_ge(q_rc, m)
                    pe.matmul(bank(4)[:, 0:T], blk, qsq[:, m % 2, :], start=True, stop=True).then_inc(q_ss, 1)
                if 2 <= n <= 10:
                    m = n - 2
                    pe.wait_ge(q_nm, m + 1)
                    if m:
                        pe.wait_ge(q_done, m)
                    pe.matmul(bank(5)[:, 0:T], cst("perm"), qnm[:, m % 2, :], start=True, stop=True).then_inc(q_rot, 1)
            pe.wait_ge(vt_ready, 1)
            for t in range(2):
                ins = pe.transpose(bank(2)[:, t * P:(t + 1) * P], vT2[:, t * P:(t + 1) * P], ident)
            ins.then_inc(v_ps2, 1)
            pe.wait_ge(q_done, 9)
            pe.wait_ge(v_ev, 1)
            for c in range(NH + 2):
                if c < 2 * WT:
                    if c >= 4 and c % 2 == 0:
                        pe.wait_ge(cv_ev, c // 2 - 1)
                    g = C0 + 2 * c
                    tile(bank(CONV_BANKS[c % 4])[:, 0:T], g, g % RING, uhc, ulc)
                if c < NH:
                    if c:
                        pe.wait_ge(lg2_used, c)
                    scores(c, QR[:, c // 2, :], KR, sc2_ps)
                if 1 <= c <= NH:
                    pe.wait_ge(pn2_ready, c)
                    if c >= 2:
                        pe.wait_ge(pt2_ready, c - 1)
                    turn_probs(c - 1, LG2[:, (c - 1) % 2, :], tp2_ps)
                if c >= 2:
                    h = c - 2
                    e = h % 2
                    pe.wait_ge(pt2_ready, h + 1)
                    if h >= 2 and e == 0:
                        pe.wait_ge(o2_ev, h // 2)
                    weigh_v(h, lambda s: VB[:, s, HD * e:HD * e + HD], PT2[:, e, :], o2_ps)
            for c in range(WT):
                if c == 0:
                    pe.wait_ge(tap, WT * (CONV_K + 1))
                ins = pe.matmul(bank(6)[:, 0:T], ones, mix2[:, c, :], start=c == 0, stop=c == WT - 1)
            ins.then_inc(ln_ps, 1)
            for c in range(WT):
                pe.wait_ge(ln_sq, c + 1)
                ins = pe.matmul(bank(7)[:, 0:T], ones, HS[:, c, :], start=c == 0, stop=c == WT - 1)
            ins.then_inc(ln_ps, 1)
            pe.wait_ge(ml_ready, 2 + WT + 2)
            for c in range(DT):
                g = BASE["out2"] + 2 * c
                if c >= 2:
                    pe.wait_ge(res_ready, 2 * DT + c - 1)
                tile(bank(c % 2)[:, 0:T], g, g % RING, lambda c: uh[:, (c + WT) % DT, :],
                     lambda c: ul[:, (c + WT) % DT, :], None if c else (ml_ready, 2 + WT + 4))
            norm_sum(4, mix2)
            for j in range(4):
                g = BASE["wq"] + 2 * j
                if j >= 2:
                    pe.wait_ge(wq_ev, j - 1)
                tile(bank(j % 2)[:, 0:T], g, g % RING, uhc, ulc, None if j else (u_ready, 5 * DT))
            loop("wq", 4, 12, wq_ev, 0)
            pe.wait_ge(wq_ev, DT)
            pe.wait_ge(s_keys, 16)
            for t in range(2):
                for n in range(2 * PH):
                    ins = pe.matmul(bank(4 * (1 - t) + n // 4)[:, (n % 4) * P:(n % 4 + 1) * P],
                                    HQ[:, n, t * P:(t + 1) * P], KEYS[:, n * NK:(n + 1) * NK], start=True, stop=True)
                ins.then_inc(sub_ps, 1)

            def gates(n, b):
                pe.wait_ge(oh_ready, n + 1)
                for t in range(4):
                    ins = pe.matmul(bank(4 + b)[:, t * 3 * QJ:(t + 1) * 3 * QJ], ROWS[:, b, t, :], COLS[:, b, t, :],
                                    start=True, stop=True)
                ins.then_inc(g_ps, 1)

            def experts_in(q, i, first=False, turn=None):
                g0 = BASE[f"u{q}"]
                for j in range(4):
                    if not first or j >= 2:
                        pe.wait_ge(u_ev, i * 4 + (QJ * q + j - 1))
                    for n in range(2):
                        g = g0 + 2 * j + n
                        unit(bank(j % 2)[:, 0:T], i * 8 + (g + 1), g % RING, lambda c: uh[:, UKT * n + c, :],
                             lambda c: ul[:, UKT * n + c, :], first=n == 0, last=n == 1).then_inc(w_used, 1)
                        if turn is not None:
                            gates(i * 8 + (EXPERT_U * turn + 2 * j + n), n % 2)

            def experts_out(q, turn=None):
                g0 = BASE[f"v{q}"]
                pe.wait_ge(u_ev, QJ * min(q + 2, NQ))
                with pe.Fori(0, DT // 2) as i:
                    for d in range(2):
                        pe.wait_ge(res_ready, i * 2 + ((3 + q) * DT + d - 1))
                        for s in range(V_U):
                            g = g0 + V_U * d + s
                            if d == 0:
                                pe.wait_ge(el_ready, 8 * q + 2 * (s + 1))
                            unit(bank(d)[:, 0:T], i * 8 + (g + 1), g % RING,
                                 lambda c: e_hi(q, UKT * s + c).rearrange("p a t -> p (a t)"),
                                 lambda c: EL[q][:, UKT * s + c, :],
                                 first=s == 0, last=s == V_U - 1).then_inc(w_used, 1)
                            if turn is not None:
                                gates(i * 8 + (EXPERT_U * turn + V_U * d + s), s % 2)

            pe.wait_ge(sub_ev, 8)
            experts_in(0, 0, first=True)
            with pe.Fori(1, 8) as i:
                experts_in(0, i)
            pe.wait_ge(route_ready, 2)
            for t in range(2):
                for n in range(3):
                    ins = pe.transpose(bank(4 + t)[:, n * P:(n + 1) * P], exs[:, t, n, :], ident)
            ins.then_inc(et_ps, 1)
            with pe.Fori(0, 8) as i:
                experts_in(1, i, turn=0)
            experts_out(0, turn=1)
            for q in range(2, NQ):
                pe.wait_ge(res_ready, (2 + q) * DT)
                with pe.Fori(0, 8) as i:
                    experts_in(q, i)
                experts_out(q - 1, turn=q)
            experts_out(NQ - 1)


        @block.scalar
        def _(act):
            act.dma_start(con[:, :], A["con"][:, 0:KEEP]).then_inc(s_con, 16)
            act.dma_start(misc[0:32, 512:528], A["table"]).then_inc(s_tab, 16)
            act.dma_start(misc[0:48, 640:1024], A["dist"]).then_inc(s_tab, 16)
            x_in = A["x"].rearrange("(c p) t -> p c t", p=P)
            for k in range(4):
                act.dma_start(xT[:, 4 * k:4 * k + 4, :], x_in[:, 4 * k:4 * k + 4, :]).then_inc(s_x[k], 16)
            act.dma_start(par[:, :], A["par"]).then_inc(s_par, 16)
            act.dma_start(arena[:, 0:TAIL], A["con"][:, KEEP:NCON]).then_inc(s_con2, 16)

            def convert(g, i=0, per=0, narrow=False):
                slot, width = g % RING, SLOT // 2 if narrow else SLOT
                act.wait_ge(w_in[slot], i * (4 * per) + 16 * (g // RING + 1))
                if g >= RING:
                    act.wait_ge(w_used, i * per + (g - RING + 1))
                act.activation(wh[:, slot, 0:width], raw[:, slot, 0:width], ACT.Copy).then_inc(hi_ready, 1)

            def ahead(g, i=0, per=0, n=2):
                for k in range(n):
                    convert(g + RING + k, i, per)

            def squares(m, sq, ready=None, before=0):
                for c in range(DT):
                    if m == 0:
                        act.wait_ge(s_x[c // 4], 16)
                    else:
                        act.wait_ge(ready, before + c + 1)
                    act.activation(sq[:, c, :], xT[:, c, :], ACT.Square).then_inc(sq_ready, 1)
                for g in (0, 1) if m == 0 else ():
                    convert(g)
                act.wait_ge(rs_ready, m + 1)
                act.activation(rstd, nrm, ACT.Sqrt).then_inc(rstd_ready, 1)
                for g in (2, 3) if m == 0 else ():
                    convert(g)

            def round_u(k):
                for c in range(0, DT, 4):
                    act.wait_ge(p_ready, 4 * k + c // 4 + 1)
                    act.activation(uh[:, c:c + 4, :], ub[:, c:c + 4, :], ACT.Copy).then_inc(uh_ready, 1)

            squares(0, ua)
            round_u(0)
            with act.Fori(0, 8) as i:
                for j in range(2):
                    ahead(2 * j, i, 4)
                    act.wait_ge(w_used, i * 4 + (2 * j + 2))
                    act.activation(QK[:, bass.ds(i * 2 + j, 1), :], ps[:, j:j + 1, 0:T], ACT.Copy)\
                        .then_inc(qkv_ev, 1)
            with act.Fori(0, 2) as i:
                for j in range(2):
                    g = 32 + 4 * j
                    ahead(g, i, 8, 4)
                    act.wait_ge(w_used, i * 8 + (g + 4))
                    act.activation(VN[:, :, bass.ds((i * 2 + j) * T, T)], ps[:, 2 * j:2 * j + 2, 0:T], ACT.Copy)\
                        .then_inc(qkv_ev, 2)

            def exps(h, logits, ready, used):
                act.wait_ge(ready, h + 1)
                s4 = small[:, 8 * (h % 2):8 * (h % 2) + 8]
                act.activation(logits[:, 0:256], logits[:, 0:256], ACT.Exp, bias=s4[:, 2:3],
                               accum_out=s4[:, 4:5])
                act.activation(logits[:, 256:384], logits[:, 256:384], ACT.Exp, bias=s4[:, 3:4],
                               accum_out=s4[:, 5:6]).then_inc(used, 1)

            for c in range(28):
                if c < 27:
                    ahead(BASE["z"] + 2 * c)
                    act.wait_ge(w_used, BASE["z"] + 2 * c + 2)
                    if c >= 2:
                        act.wait_ge(z_ready, c - 1)
                    else:
                        act.wait_ge(z_pad, 1)
                    act.activation(zraw[:, c % 2, 1:T + 1], bank(c % 2)[:, 0:T], ACT.Copy).then_inc(z_raw, 1)
                if c >= 6 and c % 3 == 0:
                    act.wait_ge(kk_rc, c // 3 - 1)
                    act.activation(sc[:, 9, :], sc[:, 11, :], ACT.Sqrt).then_inc(kk_rt, 1)
                if c < NH:
                    exps(c, LG[:, c % 2, :], lg_ready, ex_ready)
                if c == 3:
                    act.wait_ge(z_ready, 3)
                    act.activation(lo[0:64, 0, :], lo[0:64, 0, :], ACT.Tanh).then_inc(low_ready, 1)
                    act.activation(lo[:, 1, :], lo[:, 1, :], ACT.Sigmoid).then_inc(low_ready, 1)
                    act.activation(lo[0:32, 2, :], lo[0:32, 2, :], ACT.Sigmoid).then_inc(low_ready, 1)
                if 3 <= c < 27 and c % 3 == 0:
                    i = c // 3 - 1
                    act.wait_ge(lr_ps, i + 1)
                    if i:
                        act.wait_ge(bo_used, i)
                    act.activation(sc[:, 2, :], bank(6)[:, 0:T], ACT.Sigmoid, bias=prm("w0", i)).then_inc(lr_act, 1)
                    act.activation(sc[:, 3, :], bank(7)[:, T:2 * T], ACT.Sigmoid, bias=prm("a0", i))\
                        .then_inc(lr_act, 1)
                    act.activation(gT[:, i, :], bank(7)[:, 0:T], ACT.Copy).then_inc(g_ev, 1)
                if c >= 5 and c % 3 == 2:
                    i = c // 3 - 1
                    act.wait_ge(lc_ready, i + 1)
                    cut = lambda s: sc[:, s, :].rearrange("p (n t) -> p n t", n=NC_)
                    act.activation(AR[:, i, :, CH:P], cut(7), ACT.Exp)
                    act.activation(BK[:, i, :, CH:P], cut(7), ACT.Exp, scale=-1.0)
                    act.activation(AR[:, i, :, 0:CH], cut(8), ACT.Exp).then_inc(e_ready, 1)
                if 1 <= c <= NH:
                    h = c - 1
                    act.wait_ge(tp_ps, h + 1)
                    if h >= 2:
                        act.wait_ge(o_ps, h - 1)
                    act.activation(PT[:, h % 2, :], bank(3)[:, 0:384], ACT.Copy).then_inc(pt_ready, 1)
                if 2 <= c <= NH + 1 and c % 2 == 1:
                    act.wait_ge(o_ps, c - 1)
                    act.activation(attnT[:, (c - 3) // 2, :], bank(4)[:, 0:T], ACT.Copy).then_inc(o_ev, 1)

            AR4 = AR[:, :, :, :]
            QS4 = QS.rearrange("p (k e) n -> p e k n", e=2)
            for c in range(NC_):
                act.wait_ge(c_tr, c + 1)
                for b in range(2):
                    act.activation(BKn[:, 8 * b:8 * b + 8, :], bank(b).rearrange("p (h n) -> p h n", h=8), ACT.Copy)\
                        .then_inc(c_act, 1)
                for e in range(2):
                    act.activation(QS4[0:CH, e, :, :], AR4[HD * e:HD * e + HD, :, c, :], ACT.Copy)\
                        .then_inc(c_act, 1)
                act.wait_ge(v_copied, c + 1)
                act.activation(UV[CH:P, :, :], SV[CH:P, :, :], ACT.Copy).then_inc(c_act, 1)
                for n, step in enumerate(INVERSE):
                    for g in range(GROUPS):
                        half = slice(4 * g, 4 * g + 4)
                        act.wait_ge(i_ps, GROUPS * (NSTEP * c + n) + g + 1)
                        for _, _, at, evs in step:
                            for engine, to in evs:
                                if engine == "act":
                                    src = bank(at + 4 * g).rearrange("p (k n) -> p k n", k=8)
                                    act.activation(Bf[to][:, half], src[:, half], ACT.Copy).then_inc(i_act, 1)
                for g in range(GROUPS):
                    half = slice(4 * g, 4 * g + 4)
                    act.wait_ge(r_ps, GROUPS * c + g + 1)
                    act.activation(Bf[3][:, half], bank(g).rearrange("p (k n) -> p k n", k=8)[:, half], ACT.Copy)\
                        .then_inc(r_ev, 1)
                act.wait_ge(y_ps, c + 1)
                act.activation(yv[:, :, c, :], bank(6).rearrange("p (k n) -> p k n", k=8), ACT.Copy)\
                    .then_inc(y_ev, 1)

            act.dma_start(xT[:, :, :], x_in).then_inc(s_x2, 16)
            for c in (0, 4):
                act.activation(uh[:, c:c + 4, :], attnT[:, c:c + 4, :], ACT.Copy).then_inc(mh_ready, 1)

            def round_mixed(i):
                act.wait_ge(gn_out, i + 1)
                act.activation(uh[:, WT + i, :].rearrange("p (n t) -> p n t", n=NC_), yv[:, i, :, :], ACT.Copy)\
                    .then_inc(mh_ready, 1)

            for i in range(WT):
                act.wait_ge(gn_in, i + 1)
                if i >= 2:
                    act.wait_ge(gn_var, i - 1)
                act.activation(sc[:, i % 2, :].rearrange("p (n t) -> p n t", n=NC_), yv[:, i, :, :], ACT.Square)\
                    .then_inc(gn_sq, 1)
                act.wait_ge(gn_rc, i + 1)
                act.activation(sc[:, 4 + i % 2, :], sc[:, 2 + i % 2, :], ACT.Sqrt).then_inc(gn_rt, 1)

                if i:
                    round_mixed(i - 1)
            round_mixed(WT - 1)

            for c in range(DT):
                ahead(BASE["out"] + 2 * c)
            squares(1, sq1, res_ready, 0)
            round_u(1)

            def silus(i, first):
                for j in range(2):
                    g = BASE["gu"] + 4 * j
                    ahead(g, i, 8)
                    act.wait_ge(w_used, i * 8 + (g + 2))
                    if not first:
                        act.wait_ge(gu_ev, i * 2 + (j - 1))
                    act.activation(GS[:, j, :], bank(2 * j)[:, 0:T], ACT.Silu).then_inc(gs_ready, 1)
                    ahead(g + 2, i, 8)
                    act.wait_ge(gp_ready, i * 2 + (j + 1))
                    act.activation(gh[:, bass.ds(i * 2 + j, 1), :], GS[:, j:j + 1, :], ACT.Copy).then_inc(gh_ready, 1)

            silus(0, True)
            with act.Fori(1, FT // 2) as i:
                silus(i, False)
            with act.Fori(0, DT // 2) as i:
                for j in range(RING, RING + 2 * DOWN_U):
                    convert(BASE["down"] + j, i, 2 * DOWN_U, j % DOWN_U == DOWN_U - 1)
            squares(2, ua, res_ready, DT)
            squares(3, ua, u_ready, 2 * DT)
            round_u(2)
            for n in range(10):
                ahead(Q0 + 2 * n)
                if n == 1:
                    act.wait_ge(sin_in, 1)
                    act.activation(sinT, ropt[:, 1, :], ACT.Sin)
                    act.activation(cosT, posf, ACT.Sin).then_inc(sin_out, 1)
                if n < 9:
                    act.wait_ge(w_used, Q0 + 2 * n + 2)
                    if n >= 2:
                        act.wait_ge(q_nm, n - 1)
                    act.activation(qraw[:, n % 2, :], bank(n % 2)[:, 0:T], ACT.Identity, bias=prm("bin2", n))\
                        .then_inc(act_own, 1)
                    act.wait_ge(act_own, n + 1)
                    act.activation(qsq[:, n % 2, :], qraw[:, n % 2, :], ACT.Square).then_inc(q_raw, 1)
                if n >= 1:
                    act.wait_ge(q_rc, n)
                    act.activation(qsc[:, 1, :], qsc[:, 0, :], ACT.Sqrt).then_inc(q_rt, 1)
            act.wait_ge(w_used, Q0 + 20)
            act.activation(vT2, bank(1)[:, 0:T], ACT.Identity, bias=prm("bin2", 9)).then_inc(vt_ready, 1)
            act.wait_ge(v_ps2, 1)
            act.activation(VB, bank(2)[:, 0:T].rearrange("p (s n) -> p s n", s=2), ACT.Copy).then_inc(v_ev, 1)
            def round_mixed2(c, ready, n):
                act.wait_ge(ready, n)
                act.activation(uh[:, c:c + 4, :], mix2[:, c:c + 4, :], ACT.Copy).then_inc(mh_ready, 1)

            for c in range(NH + 2):
                if c < 2 * WT:
                    ahead(C0 + 2 * c)
                    if c % 2:
                        act.wait_ge(w_used, C0 + 2 * c + 2)
                        act.activation(sg[:, c // 2 % 2, :], bank(CONV_BANKS[c % 4])[:, 0:T], ACT.Sigmoid,
                                       bias=prm("bin2", 10 + c)).then_inc(sg_ready, 1)
                if c < NH:
                    act.wait_ge(lg2_ready, c + 1)
                    s4 = small[:, 16 * (c % 2):16 * (c % 2) + 16]
                    act.activation(s4[:, 8:10], s4[:, 2:4], ACT.Exp, bias=sinkr[:, c:c + 1])
                    act.activation(LG2[:, c % 2, 0:256], LG2[:, c % 2, 0:256], ACT.Exp, bias=s4[:, 2:3],
                                   accum_out=s4[:, 4:5])
                    act.activation(LG2[:, c % 2, 256:384], LG2[:, c % 2, 256:384], ACT.Exp, bias=s4[:, 3:4],
                                   accum_out=s4[:, 5:6]).then_inc(ex2_ready, 1)
                if 1 <= c <= NH:
                    h = c - 1
                    act.wait_ge(tp2_ps, h + 1)
                    if h >= 2:
                        act.wait_ge(o2_ps, h - 1)
                    act.activation(PT2[:, h % 2, :], bank(3)[:, 0:384], ACT.Copy).then_inc(pt2_ready, 1)
                if c >= 2 and c % 2 == 1:
                    act.wait_ge(o2_ps, c - 1)
                    act.activation(mix2[:, WT + (c - 3) // 2, :], bank(4)[:, 0:T], ACT.Copy).then_inc(o2_ev, 1)
            round_mixed2(WT, o2_ev, 4)
            round_mixed2(WT + 4, o2_ev, WT)
            for c in range(WT):
                act.wait_ge(ln_mid, c // 4 + 1)
                act.activation(HS[:, c, :], mix2[:, c, :], ACT.Square).then_inc(ln_sq, 1)
            act.wait_ge(ln_rc, 1)
            act.activation(rstd, nrm, ACT.Sqrt).then_inc(ln_rt, 1)
            for c in range(WT):
                act.wait_ge(ln_mul, c // 4 + 1)
                act.activation(mix2[:, c, :], mix2[:, c, :], ACT.Silu, bias=prm("clb", c), scale=prm("clg", c))\
                    .then_inc(ln_out, 1)
                if c % 4 == 3:
                    round_mixed2(c - 3, ln_out, c + 1)
            for c in range(DT):
                ahead(BASE["out2"] + 2 * c)
            squares(4, mix2, res_ready, 2 * DT)
            round_u(3)
            with act.Fori(0, 8) as i:
                for j in range(2):
                    g = BASE["wq"] + 2 * j
                    ahead(g, i, 4)
                    act.wait_ge(w_used, i * 4 + (g + 2))
                    act.activation(HQ[:, bass.ds(i * 2 + j, 1), :], ps[:, j:j + 1, 0:T], ACT.Copy)\
                        .then_inc(wq_ev, 1)
            for t in range(2):
                act.wait_ge(sub_ps, t + 1)
                for b in range(4):
                    act.activation(SUB[:, t, 4 * b:4 * b + 4, :],
                                   bank(4 * (1 - t) + b).rearrange("p (n k) -> p n k", n=4), ACT.Copy)\
                        .then_inc(sub_ev, 1)

            def gelus(q, i, round_turn=None):
                for j in range(4):
                    g = BASE[f"u{q}"] + 2 * j
                    ahead(g, i, 8)
                    act.wait_ge(w_used, i * 8 + (g + 2))
                    act.activation(HB[q][:, bass.ds(i * 4 + j, 1), :], ps[:, j % 2:j % 2 + 1, 0:T], ACT.Gelu)\
                        .then_inc(u_ev, 1)
                    if round_turn is not None:
                        round_experts(round_turn, 2 * j)
                        round_experts(round_turn, 2 * j + 1)

            def round_experts(q, k):
                act.wait_ge(gated, EXPERT_U * (q + 1))
                act.activation(e_hi(q, 4 * k, 4), HB[q][:, 4 * k:4 * k + 4, :], ACT.Copy).then_inc(eh_ready, 1)

            with act.Fori(0, 7) as i:
                gelus(0, i)
            act.wait_ge(soft_in, 2)
            for t in range(2):
                act.activation(val[:, t, :, :], val[:, t, :, :], ACT.Exp).then_inc(soft_ex, 1)
            gelus(0, 7)
            with act.Fori(0, 8) as i:
                gelus(1, i)
            for k in range(8):
                round_experts(0, k)
            for q in range(NQ):
                with act.Fori(0, DT - (q == NQ - 1)) as i:
                    ahead(BASE[f"v{q}"], i, V_U, V_U)
                if q + 2 < NQ:
                    gelus(q + 2, 0, round_turn=q + 1)
                    with act.Fori(1, 8) as i:
                        gelus(q + 2, i)
                elif q == NQ - 2:
                    for k in range(8):
                        round_experts(NQ - 1, k)


        @block.vector
        def _(dve):
            own = [0]

            def link(ins):
                own[0] += 1
                ins.then_inc(dve_own, 1)
                dve.wait_ge(dve_own, own[0])

            def bc(ap, *shape):
                return ap.unsqueeze(1).to_broadcast(list(shape))

            def scale(m, gain, k=None):
                dve.wait_ge(ss_ready, m + 1)
                link(dve.tensor_scalar(nrm, bank(2)[:, 0:T], 1.0 / D, RMS_EPS, ALU.mult, ALU.add))
                dve.reciprocal(nrm, nrm).then_inc(rs_ready, 1)
                dve.wait_ge(rstd_ready, m + 1)
                for c in range(DT):
                    ins = dve.scalar_tensor_tensor(out=(xT if k is None else ub)[:, c, :], in0=xT[:, c, :],
                                                   scalar=prm(gain, c), in1=rstd, op0=ALU.mult, op1=ALU.mult)
                    if k is None:
                        ins.then_inc(u_ready, 1)
                    elif c % 4 == 3:
                        ins.then_inc(p_ready, 1)
                        if c > 4:
                            lows(k, c - 7)
                if k is not None:
                    lows(k, DT - 4)

            def lows(k, c):
                dve.wait_ge(uh_ready, 4 * k + c // 4 + 1)
                dve.tensor_tensor(ul[:, c:c + 4, :], ub[:, c:c + 4, :], uh[:, c:c + 4, :].bitcast(F32), ALU.subtract)\
                    .then_inc(u_ready, 4)

            dve.memset(zraw[:, :, 0:1], 0.0).then_inc(z_pad, 1)
            dve.wait_ge(s_tab, 32)
            dve.wait_ge(dist_ps, 1)
            link(dve.tensor_copy(misc[0:NH, 1408:1792], misc[32:48, 640:1024]))
            dve.tensor_tensor(misc[0:NH, 1024:1408], bank(3)[0:NH, 0:384], misc[0:NH, 1408:1792], ALU.add)\
                .then_inc(dist_sb, 1)
            dve.wait_ge(s_par, 16)
            for k in range(4):
                dve.wait_ge(s_x[k], 16)
            scale(0, "n1", 0)

            def row_max(h, logits, ready):
                s4 = small[:, 8 * (h % 2):8 * (h % 2) + 8]
                dve.tensor_reduce(s4[:, 0:1], logits[:, 0:256], AX, ALU.max)
                link(dve.tensor_reduce(s4[:, 1:2], logits[:, 256:384], AX, ALU.max))
                dve.tensor_scalar(s4[:, 2:4], s4[:, 0:2], -1.0, None, ALU.mult).then_inc(ready, 1)

            def divide(h, probs, ready):
                s4 = small[:, 8 * (h % 2):8 * (h % 2) + 8]
                link(dve.reciprocal(s4[:, 6:8], s4[:, 4:6]))
                dve.tensor_scalar(probs[:, 0:256], probs[:, 0:256], s4[:, 6:7], None, ALU.mult)
                dve.tensor_scalar(probs[:, 256:384], probs[:, 256:384], s4[:, 7:8], None, ALU.mult)\
                    .then_inc(ready, 1)

            dve.wait_ge(s_con2, 16)
            r, k, lw, a, kk, sq, rkk, lc, tmp, t2, kp, rc = (sc[:, n, :] for n in range(12))

            def pair_sums(i):
                dve.wait_ge(z_ready, 3 * i + 6)
                dve.wait_ge(lr_act, 2 * i + 2)
                link(dve.tensor_scalar(lw, lw, -DECAY, None, ALU.mult))
                link(dve.tensor_tensor_scan(lc, cst("reset"), lw, 0.0, ALU.mult, ALU.add))
                dve.tensor_tensor(tmp, lc, lw, ALU.subtract).then_inc(lc_ready, 1)
                link(dve.tensor_scalar(kk, k, prm("kk", i), None, ALU.mult))
                dve.tensor_tensor(sq, kk, kk, ALU.mult).then_inc(kk_sq, 1)
                link(dve.tensor_scalar(kp, a, -1.0, prm("ka", i), ALU.add, ALU.mult))
                link(dve.scalar_tensor_tensor(out=kp, in0=kp, scalar=1.0, in1=k, op0=ALU.add, op1=ALU.mult))
                dve.scalar_tensor_tensor(out=rkk, in0=r, scalar=prm("rk", i), in1=kp, op0=ALU.mult, op1=ALU.mult)\
                    .then_inc(bo_in, 1)

            def pair_vectors(i):
                dve.wait_ge(ss_kk, i + 1)
                link(dve.tensor_scalar(rc, bank(5)[:, 0:T], 1e-24, None, ALU.max))
                dve.reciprocal(rc, rc).then_inc(kk_rc, 1)
                dve.wait_ge(e_ready, i + 1)
                cut = lambda s: s.rearrange("p (n t) -> p n t", n=NC_)
                dve.tensor_copy(wend[:, i, :].unsqueeze(2), AR[:, i, :, P - 1:P])
                dve.wait_ge(kk_rt, i + 1)
                link(dve.tensor_tensor(kk, kk, t2, ALU.mult))
                link(dve.tensor_tensor(t2, kk, a, ALU.mult))
                dve.tensor_tensor(AR[:, i, :, CH:P], AR[:, i, :, CH:P], cut(r), ALU.mult)
                dve.scalar_tensor_tensor(out=AR[:, i, :, 0:CH], in0=AR[:, i, :, 0:CH], scalar=-1.0, in1=cut(kk),
                                         op0=ALU.mult, op1=ALU.mult)
                link(dve.tensor_tensor(BK[:, i, :, 0:CH], BK[:, i, :, CH:P], cut(t2), ALU.mult))
                link(dve.tensor_tensor(BK[:, i, :, CH:P], BK[:, i, :, CH:P], cut(kp), ALU.mult))

            for c in range(28):
                if c >= 6 and c % 3 == 0:
                    pair_vectors(c // 3 - 2)
                if c < NH:
                    h = c
                    dve.wait_ge(sc_ps, h + 1)
                    dve.wait_ge(bc_in[h % 2], 32 * (h // 2 + 1))
                    if h >= 2:
                        dve.wait_ge(tp_ps, h - 1)
                    dve.scalar_tensor_tensor(out=LG[:, h % 2, :], in0=bank(2)[:, 0:384], scalar=HD ** -0.5,
                                             in1=BC[:, h % 2, :], op0=ALU.mult, op1=ALU.add).then_inc(bc_used, 1)
                    dve.wait_ge(bc_used, h + 1)
                    row_max(h, LG[:, h % 2, :], lg_ready)
                if c < 27:
                    dve.wait_ge(z_raw, c + 1)
                    if c:
                        dve.wait_ge(z_ready, c)
                    z = zraw[:, c % 2, 1:T + 1]
                    link(dve.tensor_tensor(zdif, zraw[:, c % 2, 0:T], z, ALU.subtract))
                    i = c // 3 - 1
                    dst = lo[:, c, :] if c < 3 else (sc[:, 0, :], sc[:, 1, :], vT[:, i, :])[c % 3]
                    dve.scalar_tensor_tensor(out=dst, in0=zdif, scalar=prm("mix", c), in1=z, op0=ALU.mult, op1=ALU.add)\
                        .then_inc(z_ready, 1)
                if c < NH:
                    dve.wait_ge(ex_ready, c + 1)
                    divide(c, LG[:, c % 2, :], pn_ready)
                if c >= 6 and c % 3 == 0:
                    i = c // 3 - 2
                    dve.wait_ge(bo_ps, i + 1)
                    dve.tensor_tensor(bonT[:, i, :], bank(5)[:, 0:T], vT[:, i, :], ALU.mult).then_inc(bo_used, 1)
                if c >= 5 and c % 3 == 2:
                    pair_sums(c // 3 - 1)

            wend2 = wendh.rearrange("p (k e) n -> p e k n", e=2)
            dve.tensor_copy(wend2[0:HD, 0, :, :], wend[0:HD, :, :])
            link(dve.tensor_copy(wend2[0:HD, 1, :, :], wend[HD:P, :, :]))
            MB4 = MB.rearrange("p (k e) n -> p e k n", e=2)
            QS4 = QS.rearrange("p (k e) n -> p e k n", e=2)
            UV4 = UV.rearrange("p (k e) n -> p e k n", e=2)
            cm, i64 = cst("cmask"), cst("i64")
            for c in range(NC_):
                dve.wait_ge(c_tr, c + 1)
                if c == 0:
                    dve.memset(SV[0:CH, :, :], 0.0)
                for b in range(2):
                    src = bank(2 + b)[0:CH, :].rearrange("p (h n) -> p h n", h=8)
                    ins = dve.tensor_copy(SV[CH:P, 8 * b:8 * b + 8, :], src)
                ins.then_inc(v_copied, 1)
                for e in range(2):
                    dve.wait_ge(c_ps, 3 * c + e + 1)
                    for b in range(2):
                        src = bank(4 + 2 * e + b).rearrange("p (k n) -> p k n", k=4)
                        dve.tensor_tensor(QS4[CH:P, e, 4 * b:4 * b + 4, :], src[CH:P], bc(cm[CH:P], CH, 4, P), ALU.mult)
                        ins = dve.tensor_tensor(MB4[0:CH, e, 4 * b:4 * b + 4, :], src[0:CH], bc(cm[0:CH], CH, 4, P),
                                                ALU.mult)
                link(ins)
                for e in range(2):
                    ins = dve.tensor_tensor(Bf[0][HD * e:HD * e + HD], MB4[0:CH, e, :, 0:CH],
                                            bc(cst("dmask")[0:CH], CH, 8, CH), ALU.mult)
                link(ins)
                dve.tensor_tensor(Bf[3], Bf[0], bc(i64, P, 8, CH), ALU.add)
                dve.wait_ge(c_ps, 3 * c + 3)
                dve.tensor_tensor(Bf[1], bank(0).rearrange("p (k n) -> p k n", k=8), bc(cst("dtmask"), P, 8, CH),
                                  ALU.mult).then_inc(c_dve, 1)
                for e in range(2):
                    dve.tensor_tensor(Bf[2][HD * e:HD * e + HD], MB4[0:CH, e, :, 0:CH],
                                      bc(cst("omask")[0:CH], CH, 8, CH), ALU.mult)
                for n, step in enumerate(INVERSE):
                    for g in range(GROUPS):
                        half = slice(4 * g, 4 * g + 4)
                        dve.wait_ge(i_ps, GROUPS * (NSTEP * c + n) + g + 1)
                        done = evacuated(EVA, c, n) + g * (EVA[n + 1] - EVA[n])
                        for _, _, at, evs in step:
                            for engine, to in evs:
                                src = bank(at + 4 * g).rearrange("p (k n) -> p k n", k=8)[:, half]
                                dst = Bf[to][:, half]
                                if engine == "act":
                                    copied, done = dst, done + 1
                                elif engine == "dve+":
                                    dve.wait_ge(i_act, done)
                                    dve.tensor_tensor(dst, copied, bc(i64, P, 4, CH), ALU.add).then_inc(i_dve, 1)
                                elif (n, to) in PLUS_ID:
                                    dve.tensor_tensor(dst, src, bc(i64, P, 4, CH), ALU.add).then_inc(i_dve, 1)
                                else:
                                    dve.tensor_copy(dst, src).then_inc(i_dve, 1)
                for g in range(GROUPS):
                    half = slice(4 * g, 4 * g + 4)
                    dve.wait_ge(v_ps, GROUPS * c + g + 1)
                    for e in range(2):
                        src = bank(4 - 2 * g + e)[0:CH, :].rearrange("p (k n) -> p k n", k=8)
                        ins = dve.tensor_copy(UV4[0:CH, e, half, :], src[:, half])
                    ins.then_inc(uv_ev, 1)
                if c == NC_ - 1:
                    break
                dve.wait_ge(n_ps, c + 1)
                for b in range(2):
                    src = bank(2 + b)[0:CH, :].rearrange("p (h n) -> p h n", h=8)
                    ins = dve.tensor_tensor(SV[0:CH, 8 * b:8 * b + 8, :], src, SV[0:CH, 8 * b:8 * b + 8, :], ALU.add)
                link(ins)
                dve.tensor_tensor(SV[0:CH], SV[0:CH],
                                  wendh[0:CH, :, c:c + 1].to_broadcast([CH, NH, CH]), ALU.mult).then_inc(st_ev, 1)

            def gn_finish(i):
                dve.wait_ge(gn_var, i + 1)
                v = sc[:, 2 + i % 2, :]
                link(dve.tensor_scalar(v, bank(4 + i % 2)[:, 0:T], 1.0 / HD, GN_EPS, ALU.mult, ALU.add))
                dve.reciprocal(v, v).then_inc(gn_rc, 1)
                dve.wait_ge(gn_rt, i + 1)
                y = yv[:, i, :, :]
                cut = lambda s: s.rearrange("p (n t) -> p n t", n=NC_)
                link(dve.scalar_tensor_tensor(out=y, in0=y, scalar=prm("lnw", i), in1=cut(sc[:, 4 + i % 2, :]),
                                              op0=ALU.mult, op1=ALU.mult))
                link(dve.scalar_tensor_tensor(out=y, in0=y, scalar=prm("lnb", i), in1=cut(bonT[:, i, :]),
                                              op0=ALU.add, op1=ALU.add))
                dve.tensor_tensor(y, y, cut(gT[:, i, :]), ALU.mult).then_inc(gn_out, 1)

            def mixed_low(i):
                cut = lambda s: s.rearrange("p (n t) -> p n t", n=NC_)
                dve.wait_ge(mh_ready, 2 + i + 1)
                dve.tensor_tensor(cut(ul[:, WT + i, :]), yv[:, i, :, :], cut(uh[:, WT + i, :].bitcast(F32)),
                                  ALU.subtract).then_inc(ml_ready, 1)

            dve.wait_ge(y_ev, NC_)
            for i in range(WT):
                dve.wait_ge(gn_mu, i + 1)
                mu = bank(i % 2)[:, 0:T].rearrange("p (n t) -> p n t", n=NC_)
                dve.scalar_tensor_tensor(out=yv[:, i, :, :], in0=mu, scalar=-1.0 / HD, in1=yv[:, i, :, :],
                                         op0=ALU.mult, op1=ALU.add).then_inc(gn_in, 1)
                if i:
                    gn_finish(i - 1)
                if i == 1:
                    for c in (0, 4):
                        dve.wait_ge(mh_ready, c // 4 + 1)
                        dve.tensor_tensor(ul[:, c:c + 4, :], attnT[:, c:c + 4, :], uh[:, c:c + 4, :].bitcast(F32),
                                          ALU.subtract).then_inc(ml_ready, 1)
                if i >= 2:
                    mixed_low(i - 2)
            gn_finish(WT - 1)
            mixed_low(WT - 2)
            mixed_low(WT - 1)

            dve.wait_ge(s_x2, 16)
            for c in range(DT):
                dve.wait_ge(w_used, BASE["out"] + 2 * c + 2)
                dve.tensor_tensor(xT[:, c, :], xT[:, c, :], bank(c % 2)[:, 0:T], ALU.add).then_inc(res_ready, 1)
            scale(1, "n2", 1)
            with dve.Fori(0, FT // 2) as i:
                for j in range(2):
                    dve.wait_ge(w_used, i * 8 + (BASE["gu"] + 4 * j + 4))
                    dve.wait_ge(gs_ready, i * 2 + (j + 1))
                    dve.tensor_tensor(GS[:, j:j + 1, :], ps[:, 2 * j + 1:2 * j + 2, 0:T], GS[:, j:j + 1, :], ALU.mult)\
                        .then_inc(gp_ready, 1)
                    dve.wait_ge(gh_ready, i * 2 + (j + 1))
                    at = bass.ds(i * 2 + j, 1)
                    dve.tensor_tensor(gl[:, at, :], GS[:, j:j + 1, :], gh[:, at, :].bitcast(F32), ALU.subtract)\
                        .then_inc(gu_ev, 1)
            with dve.Fori(0, DT // 2) as i:
                for j in range(2):
                    dve.wait_ge(w_used, i * (2 * DOWN_U) + (BASE["down"] + DOWN_U * (j + 1)))
                    dve.tensor_tensor(xT[:, bass.ds(i * 2 + j, 1), :], xT[:, bass.ds(i * 2 + j, 1), :],
                                      ps[:, j:j + 1, 0:T], ALU.add).then_inc(res_ready, 1)
            scale(2, "fg")
            scale(3, "n1b", 2)
            C1 = 6.28125
            C2 = round((2 * math.pi - C1) * 2 ** 21) / 2 ** 21
            C3 = 2 * math.pi - C1 - C2
            MAGIC = 1.5 * 2 ** 23
            r0, r1 = ropt[:, 0, :], ropt[:, 1, :]
            dve.wait_ge(s_con3, 16)
            dve.wait_ge(s_pos, 16)
            link(dve.tensor_copy(posf, r0.bitcast(I32)))
            link(dve.tensor_scalar(posf, posf, cst("invf"), None, ALU.mult))
            link(dve.tensor_scalar(r0, posf, 1 / (2 * math.pi), MAGIC, ALU.mult, ALU.add))
            link(dve.tensor_scalar(r0, r0, MAGIC, None, ALU.subtract))
            for part in (C1, C2, C3):
                link(dve.scalar_tensor_tensor(out=posf, in0=r0, scalar=-part, in1=posf, op0=ALU.mult, op1=ALU.add))
            link(dve.tensor_scalar(r1, posf, 3.1415925, -3.1415925, ALU.min, ALU.max))
            link(dve.tensor_scalar(r0, r1, -1.0, None, ALU.mult))
            link(dve.tensor_tensor(r0, r0, r1, ALU.max))
            dve.tensor_scalar(posf, r0, -1.0, math.pi / 2, ALU.mult, ALU.add).then_inc(sin_in, 1)
            link(dve.memset(HP[:, :, 0:PAD], 0.0))
            dve.wait_ge(sin_out, 1)

            def rotate(n):
                dve.wait_ge(q_rot, n + 1)
                a, b = qsc[:, 2, :], qsc[:, 3, :]
                dve.tensor_tensor(a, qnm[:, n % 2, :], cosT, ALU.mult)
                link(dve.tensor_tensor(b, bank(5)[:, 0:T], sinT, ALU.mult))
                dve.tensor_tensor(QR[:, n, :] if n < 8 else KR, a, b, ALU.add).then_inc(q_done, 1)
                dve.wait_ge(q_done, n + 1)

            for n in range(10):
                if n < 9:
                    dve.wait_ge(q_ss, n + 1)
                    if n:
                        dve.wait_ge(q_rt, n)
                    link(dve.tensor_scalar(qsc[:, 0, :], bank(4)[:, 0:T], 1.0 / HD, RMS_EPS, ALU.mult, ALU.add))
                    dve.reciprocal(qsc[:, 0, :], qsc[:, 0, :]).then_inc(q_rc, 1)
                    dve.wait_ge(q_rt, n + 1)
                    dve.scalar_tensor_tensor(out=qnm[:, n % 2, :], in0=qraw[:, n % 2, :],
                                             scalar=prm("qg" if n < 8 else "kg"), in1=qsc[:, 1, :],
                                             op0=ALU.mult, op1=ALU.mult).then_inc(q_nm, 1)
                if n:
                    rotate(n - 1)
            dve.wait_ge(s_sink, 16)

            def divide2(h):
                dve.wait_ge(ex2_ready, h + 1)
                s4 = small[:, 16 * (h % 2):16 * (h % 2) + 16]
                link(dve.tensor_tensor(s4[:, 4:6], s4[:, 4:6], s4[:, 8:10], ALU.add))
                link(dve.reciprocal(s4[:, 6:8], s4[:, 4:6]))
                dve.tensor_scalar(LG2[:, h % 2, 0:256], LG2[:, h % 2, 0:256], s4[:, 6:7], None, ALU.mult)
                dve.tensor_scalar(LG2[:, h % 2, 256:384], LG2[:, h % 2, 256:384], s4[:, 7:8], None, ALU.mult)\
                    .then_inc(pn2_ready, 1)

            def mixed_low2(c):
                dve.wait_ge(mh_ready, 2 + WT + (c // 4 + 2) % 4 + 1)
                dve.tensor_tensor(ul[:, c:c + 4, :], mix2[:, c:c + 4, :], uh[:, c:c + 4, :].bitcast(F32),
                                  ALU.subtract).then_inc(ml_ready, 1)

            def conv_input(p):
                dve.wait_ge(sg_ready, p + 1)
                dve.scalar_tensor_tensor(out=HP[:, p, PAD:PAD + T], in0=bank(CONV_BANKS[2 * p % 4])[:, 0:T],
                                         scalar=prm("bin2", 10 + 2 * p), in1=sg[:, p % 2, :],
                                         op0=ALU.add, op1=ALU.mult).then_inc(cv_ev, 1)
                dve.wait_ge(cv_ev, p + 1)

            def taps(p, first, last):
                for k in range(first, last):
                    dst = odd_taps if k % 2 else mix2[:, p, :]
                    src, w = HP[:, p, k:k + T], prm("cw", p * CONV_K + k)
                    before = p * (CONV_K + 1) + k - 1
                    if before > 0:
                        dve.wait_ge(tap, before)
                    if k == 0:
                        dve.tensor_scalar(dst, src, w, prm("cb", p), ALU.mult, ALU.add).then_inc(tap, 1)
                    elif k == 1:
                        dve.tensor_scalar(dst, src, w, None, ALU.mult).then_inc(tap, 1)
                    else:
                        dve.scalar_tensor_tensor(out=dst, in0=src, scalar=w, in1=dst, op0=ALU.mult, op1=ALU.add)\
                            .then_inc(tap, 1)
                if last == CONV_K:
                    dve.wait_ge(tap, p * (CONV_K + 1) + CONV_K)
                    dve.tensor_tensor(mix2[:, p, :], mix2[:, p, :], odd_taps, ALU.add).then_inc(tap, 1)

            for h in range(NH + 1):
                if h < NH:
                    dve.wait_ge(sc2_ps, h + 1)
                    if h >= 2:
                        dve.wait_ge(tp2_ps, h - 1)
                    dve.scalar_tensor_tensor(out=LG2[:, h % 2, :], in0=bank(2)[:, 0:384], scalar=HD ** -0.5,
                                             in1=cst("swa"), op0=ALU.mult, op1=ALU.add).then_inc(lg2_used, 1)
                    dve.wait_ge(lg2_used, h + 1)
                    s4 = small[:, 16 * (h % 2):16 * (h % 2) + 16]
                    dve.tensor_reduce(s4[:, 0:1], LG2[:, h % 2, 0:256], AX, ALU.max)
                    link(dve.tensor_reduce(s4[:, 1:2], LG2[:, h % 2, 256:384], AX, ALU.max))
                    dve.tensor_scalar(s4[:, 2:4], s4[:, 0:2], sinkr[:, h:h + 1], -1.0, ALU.max, ALU.mult)\
                        .then_inc(lg2_ready, 1)
                p, second = (h - 1) // 2, h % 2 == 0
                if h:
                    if not second:
                        conv_input(p)
                    taps(p, 16 if second else 0, 24 if second else 8)
                if h < NH:
                    divide2(h)
                if h:
                    taps(p, 24 if second else 8, CONV_K if second else 16)
            dve.wait_ge(ln_ps, 1)
            link(dve.tensor_scalar(nrm, bank(6)[:, 0:T], 1.0 / W, None, ALU.mult))
            for c in (0, 4):
                dve.tensor_tensor(mix2[:, c:c + 4, :], mix2[:, c:c + 4, :], bc(nrm, P, 4, T), ALU.subtract)\
                    .then_inc(ln_mid, 1)
            mixed_low2(WT)
            mixed_low2(WT + 4)
            dve.wait_ge(ln_ps, 2)
            link(dve.tensor_scalar(nrm, bank(7)[:, 0:T], 1.0 / W, RMS_EPS, ALU.mult, ALU.add))
            dve.reciprocal(nrm, nrm).then_inc(ln_rc, 1)
            dve.wait_ge(ln_rt, 1)
            for c in (0, 4):
                dve.tensor_tensor(mix2[:, c:c + 4, :], mix2[:, c:c + 4, :], bc(rstd, P, 4, T), ALU.mult)\
                    .then_inc(ln_mul, 1)
            mixed_low2(0)
            mixed_low2(4)
            for c in range(DT):
                dve.wait_ge(w_used, BASE["out2"] + 2 * c + 2)
                dve.tensor_tensor(xT[:, c, :], xT[:, c, :], bank(c % 2)[:, 0:T], ALU.add).then_inc(res_ready, 1)
            scale(4, "n2b", 3)

            def top16(values, best, index, work):
                link(dve.max(best[:, 0:8], values))
                dve.max_index(index[:, 0:8], best[:, 0:8], values)
                link(dve.match_replace(work, best[:, 0:8], values, -3.0e38))
                link(dve.max(best[:, 8:16], work))
                link(dve.max_index(index[:, 8:16], best[:, 8:16], work))

            it16 = cst("iota")[:, 0:TOPK]
            for t in range(2):
                dve.wait_ge(sub_ev, 8)
                for n in range(2 * PH):
                    top16(SUB[:, t, n, :], top[:, t, n, :], topi[:, t, n, :].bitcast(U32), wk[:, n % 2, 0:NK])
                link(dve.tensor_copy(topif[:, t, :, :], topi[:, t, :, :].bitcast(U32)))
                for h in range(PH):
                    c = cand[:, h % 2, :]
                    link(dve.tensor_tensor(c.rearrange("p (a b) -> p a b", a=TOPK),
                                           top[:, t, 2 * h, :].unsqueeze(2).to_broadcast([P, TOPK, TOPK]),
                                           top[:, t, 2 * h + 1, :].unsqueeze(1).to_broadcast([P, TOPK, TOPK]), ALU.add))
                    top16(c, val[:, t, h, :], vali[:, t, 0, h, :].bitcast(U32), wk[:, h % 2, :])
                v0, v1 = vali[:, t, 0, :, :].bitcast(U32), vali[:, t, 1, :, :].bitcast(U32)
                link(dve.tensor_scalar(v1, v0, 15, None, ALU.bitwise_and))
                link(dve.tensor_scalar(v0, v0, 4, None, ALU.logical_shift_right))
                link(dve.tensor_copy(valf[:, t, :, :, :], vali[:, t, :, :, :].bitcast(U32)))
                for h in range(PH):
                    for n in range(2):
                        p1 = pick[:, n, :, :]
                        link(dve.tensor_tensor(p1, valf[:, t, n, h, :].unsqueeze(2).to_broadcast([P, TOPK, TOPK]),
                                               it16.unsqueeze(1).to_broadcast([P, TOPK, TOPK]), ALU.is_equal))
                        link(dve.tensor_tensor(p1, p1, topif[:, t, 2 * h + n, :].unsqueeze(1)
                                               .to_broadcast([P, TOPK, TOPK]), ALU.mult))
                        link(dve.tensor_reduce(exs[:, t, n, h * TOPK:(h + 1) * TOPK], p1, AX, ALU.add))
                link(dve.tensor_copy(vsum[:, t, 0:PH].unsqueeze(2), val[:, t, :, 0:1]))
                dve.tensor_tensor(val[:, t, :, :], val[:, t, :, :],
                                  vsum[:, t, 0:PH].unsqueeze(2).to_broadcast([P, PH, TOPK]), ALU.subtract)\
                    .then_inc(soft_in, 1)
            for t in range(2):
                dve.wait_ge(soft_ex, t + 1)
                link(dve.tensor_reduce(vsum[:, t, 0:PH], val[:, t, :, :], AX, ALU.add))
                link(dve.reciprocal(vsum[:, t, PH:2 * PH], vsum[:, t, 0:PH]))
                dve.tensor_tensor(exs[:, t, 2, :].rearrange("p (h k) -> p h k", h=PH), val[:, t, :, :],
                                  vsum[:, t, PH:2 * PH].unsqueeze(2).to_broadcast([P, PH, TOPK]), ALU.mult)\
                    .then_inc(route_ready, 1)
            dve.wait_ge(et_ps, 1)
            for t in range(2):
                ins = dve.tensor_copy(eT[:, :, t * P:(t + 1) * P],
                                      bank(4 + t)[:, 0:3 * P].rearrange("p (n k) -> p n k", n=3))
            ins.then_inc(et_ev, 1)
            dve.wait_ge(et_ev, 1)
            gate32 = eT[:, 2, :]
            for k in range(3):
                link(dve.tensor_copy(GP[:, :, k:k + 1], (rest if k else gate32).unsqueeze(2)))
                if k < 2:
                    link(dve.tensor_tensor(rest.unsqueeze(2), (rest if k else gate32).unsqueeze(2), GP[:, :, k:k + 1],
                                           ALU.subtract))

            def one_hots(q, i, m):
                b = m % 2
                four = bass.ds(i * 32 + 4 * m, 4)
                wide = lambda n, w: eT[:, n, four].unsqueeze(2).to_broadcast([P, 4, w])
                dve.tensor_tensor(HITS[:, b], bc(cst("iota")[:, QJ * q:QJ * (q + 1)], P, 4, QJ), wide(1, QJ),
                                  ALU.is_equal)\
                    .then_inc(hits_ready, 1)
                dve.tensor_tensor(ROWS[:, b], bc(cst("iota"), P, 4, P), wide(0, P), ALU.is_equal)
                dve.wait_ge(hits_ready, i * 8 + (EXPERT_U * q + m + 1))
                dve.tensor_tensor(COLS[:, b].rearrange("p t (k j) -> p t k j", k=3),
                                  HITS[:, b].unsqueeze(2).to_broadcast([P, 4, 3, QJ]),
                                  GP[:, four, :].unsqueeze(3).to_broadcast([P, 4, 3, QJ]), ALU.mult)\
                    .then_inc(oh_ready, 1)

            def gate(q, i, m, last):
                if m < 7 or not last:
                    one_hots(q, i, m + 1)
                dve.wait_ge(g_ps, i * 8 + (EXPERT_U * q + m + 1))
                parts = bank(4 + m % 2)[:, 0:3 * P].rearrange("p (t k j) -> p t j k", t=4, k=3)
                dve.tensor_reduce(SUMS[:, m % 2], parts, AX, ALU.add).then_inc(sums_ready, 1)
                dve.wait_ge(sums_ready, i * 8 + (EXPERT_U * q + m + 1))
                h4 = HB[q][:, :, bass.ds(i * 32 + 4 * m, 4)].rearrange("p j t -> p t j")
                dve.tensor_tensor(h4, h4, SUMS[:, m % 2], ALU.mult).then_inc(gated, 1)

            def expert_lows(q):
                for k in range(8):
                    dve.wait_ge(eh_ready, 8 * q + k + 1)
                    dve.tensor_tensor(EL[q][:, 4 * k:4 * k + 4, :], HB[q][:, 4 * k:4 * k + 4, :],
                                      e_hi(q, 4 * k, 4).bitcast(F32), ALU.subtract).then_inc(el_ready, 1)

            dve.wait_ge(u_ev, QJ)
            one_hots(0, 0, 0)
            with dve.Fori(0, 7) as i:
                for m in range(8):
                    gate(0, i, m, False)
            for m in range(8):
                gate(0, 7, m, True)
            expert_lows(0)

            def add_out(q, i, last):
                for d in range(2):
                    for s in range(V_U) if q < NQ - 1 else ():
                        gate(q + 1, i, V_U * d + s, last)
                    dve.wait_ge(w_used, i * 8 + (BASE[f"v{q}"] + V_U * (d + 1)))
                    x = xT[:, bass.ds(i * 2 + d, 1), :]
                    dve.tensor_tensor(x, x, ps[:, d:d + 1, 0:T], ALU.add).then_inc(res_ready, 1)

            for q in range(NQ):
                if q < NQ - 1:
                    dve.wait_ge(u_ev, QJ * (q + 2))
                    one_hots(q + 1, 0, 0)
                with dve.Fori(0, 7) as i:
                    add_out(q, i, False)
                add_out(q, 7, True)
                if q < NQ - 1:
                    expert_lows(q + 1)


def units(w):
    k, n = w.shape
    q = k // SLOT
    return np.ascontiguousarray(w.reshape(q, UKT, P, n // P, P).transpose(3, 0, 2, 1, 4).reshape(-1, P, SLOT))


def wide_units(w):
    k, n = w.shape
    return np.ascontiguousarray(w.reshape(k // (4 * P), 4, P, n // T, T).transpose(3, 0, 2, 1, 4).reshape(-1, P, SLOT))


def columns(v, tiles):
    v = np.asarray(v).reshape(-1)
    return v.reshape(tiles, P).T


def lay_out(x):
    f = lambda n: np.asarray(x[n])
    out = {"x": f("x")[0].T, "con": constants(), "dist": distance_constants(), "table": f("rel_bias_table"),
           "w_up": f("rwkv_w_up")[0], "a_up": f("rwkv_a_up")[0], "g_up": f("rwkv_g_up")[0]}
    w_in = f("w_in")[0]
    out["w_qkv"] = np.concatenate([units(w_in[:, :2 * W]), wide_units(w_in[:, 2 * W:3 * W])], 0)
    order = np.concatenate([np.arange(3 * W, 3 * W + 128)] +
                           [g * W + np.arange(i * P, (i + 1) * P) for i in range(WT) for g in range(3)])
    gate = 3 * W + 128 + np.arange(160)

    def z_columns(m):
        pad = np.zeros((m.shape[0], 96), np.float32)
        return np.concatenate([m[:, order[:128]], m[:, gate], pad, m[:, order[128:]]], 1)

    out["w_z"] = units(z_columns(w_in[:, 3 * W:]))
    mix = z_columns(f("rwkv_shift_mix"))[0]
    out["w_out"] = units(f("w_out")[0])
    gu = f("w_gate_up")[0].reshape(D, 2, FT, P).transpose(0, 2, 1, 3).reshape(D, 2 * FFN)
    out["w_gu"] = units(gu)
    down = f("w_down")[0]
    out["w_down"] = units(np.concatenate([down, np.zeros((DOWN_U * SLOT - FFN, D), np.float32)], 0))
    heads = np.array([h for i in range(8) for h in (i, i + 8)])
    q_cols = (heads[:, None] * HD + np.arange(HD)).reshape(-1)
    conv = np.arange(2 * W).reshape(2, WT, P).transpose(1, 0, 2).reshape(-1)
    cols = np.concatenate([2 * W + q_cols, np.arange(3 * W, 3 * W + 256), conv])
    out["w_in2"] = units(f("w_in_2")[:, cols])
    b_in = f("b_in_2")[cols]
    w_out2 = f("w_out_2")
    out["w_out2"] = units(np.concatenate([w_out2[W:][q_cols], w_out2[:W]], 0))
    out["sinks"] = f("attn_sinks_2")[heads][None, :]
    out["pos"] = f("positions_2")
    out["w_wq"] = units(f("peer_w_q_2"))
    out["keys"] = f("peer_sub_keys_2").transpose(3, 0, 1, 2).reshape(P, 2 * PH * NK)
    u = f("peer_u_2").reshape(NK, NK, 2, UKT, P).transpose(1, 2, 4, 3, 0)
    out["w_u"] = np.ascontiguousarray(u).reshape(2 * NK, P, SLOT)
    v = f("peer_v_2").reshape(NK, NQ, V_U, UKT, DT, P).transpose(1, 4, 2, 0, 3, 5)
    out["w_v"] = np.ascontiguousarray(v).reshape(NQ * DT * V_U, P, SLOT)
    vec = {"n1": f("norm1_g"), "n2": f("norm2_g"), "fg": f("final_g"), "n1b": f("norm1_g_2"), "n2b": f("norm2_g_2"),
           "mix": mix, "w0": f("rwkv_w0"), "a0": f("rwkv_a0"), "kk": f("rwkv_k_k"), "ka": f("rwkv_k_a"),
           "rk": f("rwkv_r_k"), "lnw": f("rwkv_ln_w"), "lnb": f("rwkv_ln_b"), "bin2": b_in,
           "cb": f("conv_dw_b_2"), "clg": f("conv_ln_g_2"), "clb": f("conv_ln_b_2")}
    parts = []
    for name, n in PARAMS:
        if name == "cw":
            parts.append(f("conv_dw_w_2").reshape(CONV_K, WT, P).transpose(2, 1, 0).reshape(P, WT * CONV_K))
        elif name in ("qg", "kg"):
            g = f("q_norm_g_2" if name == "qg" else "k_norm_g_2")
            parts.append(np.concatenate([g, g])[:, None])
        else:
            parts.append(columns(vec[name], n))
    out["par"] = np.concatenate(parts, 1)
    return {k: np.ascontiguousarray(v) for k, v in out.items()}


def kernel(**inputs):
    import concourse.bacc as bacc
    from concourse.bass_utils import run_bass_kernel_spmd

    arrays = lay_out(inputs)
    nc = bacc.Bacc("TRN2", target_bir_lowering=False, num_devices=1)
    A = {k: nc.dram_tensor(k, a.shape, mybir.dt.from_np(a.dtype), kind="ExternalInput").ap()
         for k, a in arrays.items()}
    A["y"] = nc.dram_tensor("y", (D, T), F32, kind="ExternalOutput").ap()
    build(nc, A)
    r = run_bass_kernel_spmd(nc, [arrays], core_ids=[0])
    return np.ascontiguousarray(r.results[0]["y"].T).reshape(1, T, D)
```
